# Optimizing a Trainium2 kernel written in Bass

```python
import math
import jax, jax.numpy as jnp
from jax import lax
import numpy as np

D_MODEL = 1024
BATCH = 1
SEQ = 256
DEPTH = 2

CTX_LEN = 256
GRID_W = 64
CHUNK = 64
CONV_W = 5
EPS = 1e-6

SSD_HEAD_DIM = 64
SSD_INNER = D_MODEL
SSD_HEADS = SSD_INNER // SSD_HEAD_DIM
SSD_GROUPS = 2
SSD_STATE = 128
SSD_CONV_DIM = SSD_INNER + 2 * SSD_GROUPS * SSD_STATE

GLA_HEADS = 4
GLA_KEY = D_MODEL // 2
GLA_VAL = D_MODEL
GLA_DK = GLA_KEY // GLA_HEADS
GLA_DV = GLA_VAL // GLA_HEADS
GLA_GATE_RANK = 16
GLA_GATE_NORM = 16.0

GDN_DK = 128
GDN_DV = 128
GDN_QK_HEADS = D_MODEL // GDN_DK
GDN_V_HEADS = 2 * GDN_QK_HEADS
GDN_KEY = GDN_QK_HEADS * GDN_DK
GDN_VAL = GDN_V_HEADS * GDN_DV
GDN_CONV_DIM = 2 * GDN_KEY + GDN_VAL

D_FF = ((8 * D_MODEL + 3 * 256 - 1) // (3 * 256)) * 256

EV_SPLITS = (SSD_INNER, SSD_CONV_DIM, SSD_HEADS, SSD_HEADS,
             GLA_KEY, GLA_KEY, GLA_VAL, GLA_VAL, GLA_GATE_RANK, GLA_GATE_RANK)
EV_IN = sum(EV_SPLITS)
EV_OUT = SSD_INNER + GLA_VAL
OD_SPLITS = (GDN_CONV_DIM, GDN_VAL, GDN_V_HEADS, GDN_V_HEADS, GDN_V_HEADS, GDN_V_HEADS)
OD_IN = sum(OD_SPLITS)
OD_OUT = GDN_VAL

kernel_name = "hybrid_ssd_gla_gdn_prefix_ctx_block"

def split_cols(y, sizes):
    idx, acc = [], 0
    for s in sizes[:-1]:
        acc += s
        idx.append(acc)
    return jnp.split(y, idx, axis=-1)

def rms_norm(x, w):
    xf = x.astype(jnp.float32)
    y = xf * lax.rsqrt(jnp.mean(xf * xf, axis=-1, keepdims=True) + EPS)
    return (y * w).astype(x.dtype)

def l2_normalize(x):
    return x * lax.rsqrt(jnp.sum(x * x, axis=-1, keepdims=True) + EPS)

def centred_conv(x, w, b=None):
    pad = CONV_W // 2
    y = lax.conv_general_dilated(x, w[:, None, :].astype(x.dtype), (1,), [(pad, pad)],
                                 dimension_numbers=('NWC', 'WIO', 'NWC'),
                                 feature_group_count=x.shape[-1])
    return y if b is None else y + b

def swiglu(h, w1, w3, w2):
    return (jax.nn.silu(h @ w1) * (h @ w3)) @ w2

def to_column_major(h):
    b, t, d = h.shape
    rows = t // GRID_W
    return h.reshape(b, rows, GRID_W, d).transpose(0, 2, 1, 3).reshape(b, t, d)

def from_column_major(h):
    b, t, d = h.shape
    rows = t // GRID_W
    return h.reshape(b, GRID_W, rows, d).transpose(0, 2, 1, 3).reshape(b, t, d)

def ssd_scan(xdt, da, bm, cm, s0):
    b, t, h, p = xdt.shape
    g, n = bm.shape[2:]
    e = h // g
    nc = t // CHUNK
    tril = jnp.tril(jnp.ones((CHUNK, CHUNK), bool))
    xc = xdt.reshape(b, nc, CHUNK, g, e, p)
    ac = jnp.cumsum(da.reshape(b, nc, CHUNK, g, e), axis=2)
    bc = bm.reshape(b, nc, CHUNK, g, n)
    cc = cm.reshape(b, nc, CHUNK, g, n)
    seg = ac[:, :, :, None] - ac[:, :, None]
    decay = jnp.exp(jnp.where(tril[:, :, None, None], seg, -jnp.inf))
    scores = jnp.einsum('bclgn,bcsgn->bclsg', cc, bc)[..., None] * decay
    y_diag = jnp.einsum('bclsge,bcsgep->bclgep', scores, xc)
    to_end = jnp.exp(ac[:, :, -1:] - ac)
    states = jnp.einsum('bclgn,bclgep->bcgepn', bc, xc * to_end[..., None])
    chunk_decay = jnp.exp(ac[:, :, -1])

    def step(s, inp):
        dec, st = inp
        return dec[..., None, None] * s + st, s

    s_final, s_start = lax.scan(step, s0, (jnp.moveaxis(chunk_decay, 1, 0), jnp.moveaxis(states, 1, 0)))
    s_start = jnp.moveaxis(s_start, 0, 1)
    y_off = jnp.einsum('bclgn,bcgepn->bclgep', cc, s_start) * jnp.exp(ac)[..., None]
    return (y_diag + y_off).reshape(b, t, h, p), s_final

def gla_scan(q, k, v, gk, s0):
    b, t, h, dk = q.shape
    dv = v.shape[-1]
    nc = t // CHUNK
    tril = jnp.tril(jnp.ones((CHUNK, CHUNK), bool))

    def chunks(a):
        return a.reshape(b, nc, CHUNK, h, a.shape[-1]).transpose(1, 0, 3, 2, 4)

    def step(s, inp):
        qc, kc, vc, gc = inp
        gcum = jnp.cumsum(gc, axis=2)
        rel = jnp.exp(jnp.where(tril[:, :, None], gcum[:, :, :, None] - gcum[:, :, None], -jnp.inf))
        att = jnp.einsum('bhld,bhlsd->bhls', qc, rel * kc[:, :, None])
        o = (jnp.einsum('bhls,bhsv->bhlv', att, vc)
             + jnp.einsum('bhld,bhdv->bhlv', qc * jnp.exp(gcum), s))
        glast = gcum[:, :, -1:]
        s = (jnp.exp(glast[:, :, 0])[..., None] * s
             + jnp.einsum('bhld,bhlv->bhdv', kc * jnp.exp(glast - gcum), vc))
        return s, o

    s_final, o = lax.scan(step, s0, (chunks(q), chunks(k), chunks(v), chunks(gk)))
    return o.transpose(1, 0, 3, 2, 4).reshape(b, t, h, dv), s_final

def gdn_scan(q, k, v, g, beta, s0):
    b, t, h, dk = q.shape
    dv = v.shape[-1]
    nc = t // CHUNK
    tril = jnp.tril(jnp.ones((CHUNK, CHUNK), bool))
    strict = jnp.tril(jnp.ones((CHUNK, CHUNK), bool), -1)
    eye = jnp.eye(CHUNK, dtype=jnp.float32)

    def chunks(a):
        return a.reshape(b, nc, CHUNK, h, a.shape[-1]).transpose(0, 1, 3, 2, 4)

    qc, kc, vc = chunks(q), chunks(k), chunks(v)
    gcum = jnp.cumsum(g.reshape(b, nc, CHUNK, h).transpose(0, 1, 3, 2), axis=-1)
    bc = beta.reshape(b, nc, CHUNK, h).transpose(0, 1, 3, 2)
    decay = jnp.exp(jnp.where(tril, gcum[..., :, None] - gcum[..., None, :], -jnp.inf))
    kb = kc * bc[..., None]
    a_mat = jnp.where(strict, jnp.einsum('bchld,bchsd->bchls', kb, kc) * decay, 0.0)
    t_inv = lax.linalg.triangular_solve(eye + a_mat, jnp.broadcast_to(eye, a_mat.shape),
                                        left_side=True, lower=True, unit_diagonal=True)
    u = t_inv @ (vc * bc[..., None])
    w = t_inv @ (kb * jnp.exp(gcum)[..., None])
    att = jnp.einsum('bchld,bchsd->bchls', qc, kc) * decay
    q_dec = qc * jnp.exp(gcum)[..., None]
    k_dec = kc * jnp.exp(gcum[..., -1:] - gcum)[..., None]
    g_last = jnp.exp(gcum[..., -1])

    def step(s, inp):
        u_c, w_c, att_c, qd_c, kd_c, gl_c = inp
        v_new = u_c - jnp.einsum('bhld,bhdv->bhlv', w_c, s)
        o = jnp.einsum('bhld,bhdv->bhlv', qd_c, s) + jnp.einsum('bhls,bhsv->bhlv', att_c, v_new)
        s = gl_c[..., None, None] * s + jnp.einsum('bhld,bhlv->bhdv', kd_c, v_new)
        return s, o

    xs = tuple(jnp.moveaxis(a, 1, 0) for a in (u, w, att, q_dec, k_dec, g_last))
    s_final, o = lax.scan(step, s0, xs)
    return o.transpose(1, 0, 3, 2, 4).reshape(b, t, h, dv), s_final

def _flip(ts):
    return tuple(jnp.flip(a, axis=1) for a in ts)

def bidirectional(core, ctx_f, lat_f, ctx_b, lat_b, s0, need_ctx):
    oc_f, sc_f = core(*ctx_f, s0)
    ol_f, _ = core(*lat_f, sc_f)
    oc_b, sc_b = core(*_flip(ctx_b), s0)
    ol_b, _ = core(*_flip(lat_b), sc_b)
    ol = ol_f + jnp.flip(ol_b, axis=1)
    oc = oc_f + jnp.flip(oc_b, axis=1) if need_ctx else None
    return oc, ol

def even_mixer(hc, hl, w_in, conv_w, conv_b, dt_bias, a_log, d_skip, ssd_nw, gate_w, gate_b, gla_nw, w_out, need_ctx):
    f32 = jnp.float32
    a_neg = -jnp.exp(a_log.astype(f32))

    def project(h):
        b, t, _ = h.shape
        z, xbc, dt_f, dt_b, q, k, v, r, gl_f, gl_b = split_cols(h @ w_in, EV_SPLITS)
        xbc = jax.nn.silu(centred_conv(xbc, conv_w, conv_b)).astype(f32)
        xs, bm, cm = split_cols(xbc, (SSD_INNER, SSD_GROUPS * SSD_STATE, SSD_GROUPS * SSD_STATE))
        xs = xs.reshape(b, t, SSD_HEADS, SSD_HEAD_DIM)
        bm = bm.reshape(b, t, SSD_GROUPS, SSD_STATE)
        cm = cm.reshape(b, t, SSD_GROUPS, SSD_STATE)
        dt_f = jax.nn.softplus(dt_f.astype(f32) + dt_bias[0])
        dt_b = jax.nn.softplus(dt_b.astype(f32) + dt_bias[1])
        ssd_f = (xs * dt_f[..., None], dt_f * a_neg[0], bm, cm)
        ssd_b = (xs * dt_b[..., None], dt_b * a_neg[1], bm, cm)
        q = q.astype(f32).reshape(b, t, GLA_HEADS, GLA_DK) * GLA_DK ** -0.5
        k = k.astype(f32).reshape(b, t, GLA_HEADS, GLA_DK)
        v = v.astype(f32).reshape(b, t, GLA_HEADS, GLA_DV)
        gk_f = (jax.nn.log_sigmoid((gl_f @ gate_w[0] + gate_b[0]).astype(f32)) / GLA_GATE_NORM).reshape(b, t, GLA_HEADS, GLA_DK)
        gk_b = (jax.nn.log_sigmoid((gl_b @ gate_w[1] + gate_b[1]).astype(f32)) / GLA_GATE_NORM).reshape(b, t, GLA_HEADS, GLA_DK)
        return ssd_f, ssd_b, (q, k, v, gk_f), (q, k, v, gk_b), (xs, z, r)

    def merge(y_ssd, y_gla, aux):
        xs, z, r = aux
        b, t = z.shape[:2]
        y = (y_ssd + d_skip[:, None] * xs).reshape(b, t, SSD_INNER) * jax.nn.silu(z)
        y = rms_norm(y.reshape(b, t, SSD_GROUPS, SSD_INNER // SSD_GROUPS),
                     ssd_nw.reshape(SSD_GROUPS, SSD_INNER // SSD_GROUPS)).reshape(b, t, SSD_INNER)
        o = rms_norm(y_gla, gla_nw).reshape(b, t, GLA_VAL) * jax.nn.silu(r)
        return jnp.concatenate([y, o], axis=-1) @ w_out

    pc, pl = project(hc), project(hl)
    b = hl.shape[0]
    s0_ssd = jnp.zeros((b, SSD_GROUPS, SSD_HEADS // SSD_GROUPS, SSD_HEAD_DIM, SSD_STATE), f32)
    ssd_c, ssd_l = bidirectional(ssd_scan, pc[0], pl[0], pc[1], pl[1], s0_ssd, need_ctx)
    s0_gla = jnp.zeros((b, GLA_HEADS, GLA_DK, GLA_DV), f32)
    gla_c, gla_l = bidirectional(gla_scan, pc[2], pl[2], pc[3], pl[3], s0_gla, need_ctx)
    out_l = merge(ssd_l, gla_l, pl[4])
    out_c = merge(ssd_c, gla_c, pc[4]) if need_ctx else None
    return out_c, out_l

def odd_mixer(hc, hl, w_in, conv_w, dt_bias, a_log, gdn_nw, w_out, need_ctx):
    f32 = jnp.float32
    a_pos = jnp.exp(a_log.astype(f32))
    rep = GDN_V_HEADS // GDN_QK_HEADS

    def project(h):
        b, t, _ = h.shape
        qkv, z, a_f, a_b, b_f, b_b = split_cols(h @ w_in, OD_SPLITS)
        qkv = jax.nn.silu(centred_conv(qkv, conv_w)).astype(f32)
        q, k, v = split_cols(qkv, (GDN_KEY, GDN_KEY, GDN_VAL))
        q = jnp.repeat(l2_normalize(q.reshape(b, t, GDN_QK_HEADS, GDN_DK)) * GDN_DK ** -0.5, rep, axis=2)
        k = jnp.repeat(l2_normalize(k.reshape(b, t, GDN_QK_HEADS, GDN_DK)), rep, axis=2)
        v = v.reshape(b, t, GDN_V_HEADS, GDN_DV)
        g_f = -a_pos[0] * jax.nn.softplus(a_f.astype(f32) + dt_bias[0])
        g_b = -a_pos[1] * jax.nn.softplus(a_b.astype(f32) + dt_bias[1])
        beta_f = jax.nn.sigmoid(b_f.astype(f32))
        beta_b = jax.nn.sigmoid(b_b.astype(f32))
        return (q, k, v, g_f, beta_f), (q, k, v, g_b, beta_b), z

    def merge(o, z):
        b, t = z.shape[:2]
        o = rms_norm(o, gdn_nw) * jax.nn.silu(z.reshape(b, t, GDN_V_HEADS, GDN_DV))
        return o.reshape(b, t, GDN_VAL) @ w_out

    pc, pl = project(hc), project(hl)
    s0 = jnp.zeros((hl.shape[0], GDN_V_HEADS, GDN_DK, GDN_DV), f32)
    oc, ol = bidirectional(gdn_scan, pc[0], pl[0], pc[1], pl[1], s0, need_ctx)
    out_l = merge(ol, pl[2])
    out_c = merge(oc, pc[2]) if need_ctx else None
    return out_c, out_l

def setup_inputs(seed: int = 0) -> dict:
    key = jax.random.key(seed)
    ks = iter(jax.random.split(key, 40))
    n_ev = (DEPTH + 1) // 2
    n_od = DEPTH // 2

    def nrm(shape, scale):
        return scale * jax.random.normal(next(ks), shape, jnp.float32)

    def gain(shape):
        return 1.0 + 0.02 * jax.random.normal(next(ks), shape, jnp.float32)

    def dt_bias(shape):
        dt = jnp.exp(jax.random.uniform(next(ks), shape, jnp.float32, math.log(1e-3), math.log(1e-1)))
        return dt + jnp.log(-jnp.expm1(-dt))

    def a_log(shape):
        return jnp.log(jax.random.uniform(next(ks), shape, jnp.float32, 1.0, 16.0))

    return {
        "x": nrm((BATCH, SEQ, D_MODEL), 1.0),
        "c": nrm((BATCH, D_MODEL), 1.0),
        "ctx": nrm((BATCH, CTX_LEN, D_MODEL), 1.0),
        "c_ctx": nrm((D_MODEL,), 1.0),
        "mod_w": nrm((DEPTH, D_MODEL, 6 * D_MODEL), 0.5 * D_MODEL ** -0.5),
        "mod_b": nrm((DEPTH, 6 * D_MODEL), 0.02),
        "norm_mix": gain((DEPTH, D_MODEL)),
        "norm_ffn": gain((DEPTH, D_MODEL)),
        "ffn_w1": nrm((DEPTH, D_MODEL, D_FF), D_MODEL ** -0.5),
        "ffn_w3": nrm((DEPTH, D_MODEL, D_FF), D_MODEL ** -0.5),
        "ffn_w2": nrm((DEPTH, D_FF, D_MODEL), D_FF ** -0.5),
        "ev_w_in": nrm((n_ev, D_MODEL, EV_IN), D_MODEL ** -0.5),
        "ssd_conv_w": nrm((n_ev, CONV_W, SSD_CONV_DIM), CONV_W ** -0.5),
        "ssd_conv_b": nrm((n_ev, SSD_CONV_DIM), 0.02),
        "ssd_dt_bias": dt_bias((n_ev, 2, SSD_HEADS)),
        "ssd_a_log": a_log((n_ev, 2, SSD_HEADS)),
        "ssd_d": gain((n_ev, SSD_HEADS)),
        "ssd_norm": gain((n_ev, SSD_INNER)),
        "gla_gate_w": nrm((n_ev, 2, GLA_GATE_RANK, GLA_KEY), GLA_GATE_RANK ** -0.5),
        "gla_gate_b": nrm((n_ev, 2, GLA_KEY), 0.02),
        "gla_norm": gain((n_ev, GLA_DV)),
        "ev_w_out": nrm((n_ev, EV_OUT, D_MODEL), EV_OUT ** -0.5),
        "od_w_in": nrm((n_od, D_MODEL, OD_IN), D_MODEL ** -0.5),
        "gdn_conv_w": nrm((n_od, CONV_W, GDN_CONV_DIM), CONV_W ** -0.5),
        "gdn_dt_bias": dt_bias((n_od, 2, GDN_V_HEADS)),
        "gdn_a_log": a_log((n_od, 2, GDN_V_HEADS)),
        "gdn_norm": gain((n_od, GDN_DV)),
        "od_w_out": nrm((n_od, OD_OUT, D_MODEL), OD_OUT ** -0.5),
        "final_norm": gain((D_MODEL,)),
    }

def reference(x, c, ctx, c_ctx, mod_w, mod_b, norm_mix, norm_ffn, ffn_w1, ffn_w3, ffn_w2,
              ev_w_in, ssd_conv_w, ssd_conv_b, ssd_dt_bias, ssd_a_log, ssd_d, ssd_norm,
              gla_gate_w, gla_gate_b, gla_norm, ev_w_out,
              od_w_in, gdn_conv_w, gdn_dt_bias, gdn_a_log, gdn_norm, od_w_out, final_norm):
    xc = ctx
    for i in range(DEPTH):
        last = i == DEPTH - 1
        j = i // 2
        sh1, sc1, g1, sh2, sc2, g2 = (m[:, None, :] for m in jnp.split(jax.nn.silu(c) @ mod_w[i] + mod_b[i], 6, axis=-1))
        ch1, cs1, cg1, ch2, cs2, cg2 = jnp.split(jax.nn.silu(c_ctx) @ mod_w[i] + mod_b[i], 6, axis=-1)
        hl = rms_norm(x, norm_mix[i]) * (1.0 + sc1) + sh1
        hc = rms_norm(xc, norm_mix[i]) * (1.0 + cs1) + ch1
        if i % 2 == 0:
            yc, yl = even_mixer(hc, hl, ev_w_in[j], ssd_conv_w[j], ssd_conv_b[j], ssd_dt_bias[j], ssd_a_log[j],
                                ssd_d[j], ssd_norm[j], gla_gate_w[j], gla_gate_b[j], gla_norm[j], ev_w_out[j],
                                not last)
        else:
            yc, yl = odd_mixer(hc, to_column_major(hl), od_w_in[j], gdn_conv_w[j], gdn_dt_bias[j], gdn_a_log[j],
                               gdn_norm[j], od_w_out[j], not last)
            yl = from_column_major(yl)
        x = x + g1 * yl
        x = x + g2 * swiglu(rms_norm(x, norm_ffn[i]) * (1.0 + sc2) + sh2, ffn_w1[i], ffn_w3[i], ffn_w2[i])
        if not last:
            xc = xc + cg1 * yc
            xc = xc + cg2 * swiglu(rms_norm(xc, norm_ffn[i]) * (1.0 + cs2) + ch2, ffn_w1[i], ffn_w3[i], ffn_w2[i])
    return rms_norm(x, final_norm)


_drawn_inputs = setup_inputs


def setup_inputs(seed=0):
    import zlib

    import numpy as np

    out = dict(_drawn_inputs(seed))
    spreads = {}
    factors = {'norm_mix': 5.458,
     'norm_ffn': 6.742,
     'ssd_conv_b': 31.154,
     'ssd_d': 64.0,
     'ssd_norm': 51.358,
     'gla_gate_b': 8.0,
     'gla_norm': 8.0,
     'gdn_norm': 37.018,
     'final_norm': 7.352}
    for name, (base, spread) in spreads.items():
        noise = np.random.default_rng([zlib.crc32(name.encode()), seed]).standard_normal(out[name].shape)
        drawn = base * np.exp(spread * noise) if base else spread * noise
        out[name] = __import__('jax').numpy.asarray(drawn.astype(out[name].dtype))
    for name, factor in factors.items():
        out[name] = (out[name] * factor).astype(out[name].dtype)
    return out
```

```python
from contextlib import ExitStack

import numpy as np

import concourse.bass as bass
from concourse import mybir

P = 128
F32 = mybir.dt.float32
ALU = mybir.AluOpType
ACT = mybir.ActivationFunctionType
AX_X = mybir.AxisListType.X

D = 1024
KC = D // P
CTX = 256
LAT = 256
T = CTX + LAT
TT = T // P
GRID_W = 64
ROWS = LAT // GRID_W
TAPS = 5
PAD = TAPS // 2
EPS = 1e-6
D_FF = ((8 * D + 3 * 256 - 1) // (3 * 256)) * 256
FC = D_FF // P
SSD_H = 16
SSD_P = 64
SSD_G = 2
GHP = SSD_H // SSD_G * SSD_P
GLA_H = 4
GLA_DK = 128
GLA_DV = 256
GLA_NORM = 16.0
RANK = 16
QK_H = 8
GDN_DK = 128
GDN_DV = 128
V_H = 16
CB = 256
RING = 3
LEV = 7
XBC_T = (D + 2 * SSD_G * P) // P
EV = {"z": 0, "xbc": 1024, "dt": 2560, "q": 2592, "k": 3104, "v": 3616, "r": 4640, "gl": 5664}
OD = {"q": 0, "k": 1024, "v": 2048, "z": 4096, "ab": 6144}
DIRS = (0, 1)
TILE_AT = ((0, 1, 2, 3), (1, 0, 3, 2))

COLS = {}


def _cols():
    at = 0
    for name, n in (("c", 2 * KC), ("norm_mix", 2 * KC), ("norm_ffn", 2 * KC), ("final", KC),
                    ("mod_b", 2 * 48), ("conv_w0", XBC_T * TAPS), ("conv_b0", XBC_T),
                    ("conv_w1", 32 * TAPS), ("ssd_norm", KC), ("gla_norm", 2), ("gdn_norm", 1)):
        COLS[name] = (at, n)
        at += n
    return at


NCOL = _cols()
ROWV = {"dtb0": 0, "alog0": 32, "dskip": 64, "dtb1": 80, "alog1": 112}
NROW = 144
CI = {"ident": 0, "ones": 1, "le": 2, "ge": 3, "gt": 4, "lt": 5, "lvl0": 6, "lvl1": 14, "msk0": 22, "msk1": 30, "pick": 38}
NCONST = 39


def constants():
    t = np.arange(P)[:, None]
    x = np.arange(P)[None, :]
    out = np.zeros((P, NCONST, P), np.float32)
    out[:, CI["ident"]] = t == x
    out[:, CI["ones"]] = 1
    out[:, CI["le"]] = t <= x
    out[:, CI["ge"]] = t >= x
    out[:, CI["gt"]] = t > x
    out[:, CI["lt"]] = t < x
    for b in range(LEV):
        same = (t >> b) == (x >> b)
        high = ((x >> b) & 1) == 1
        out[:, CI["lvl0"] + b] = same & np.where(high, t <= x, t > x)
        out[:, CI["lvl1"] + b] = same & np.where(high, t < x, t >= x)
        pair = (t >> (b + 1)) == (x >> (b + 1))
        t_high = ((t >> b) & 1) == 1
        out[:, CI["msk0"] + b] = pair & ~t_high & high
        out[:, CI["msk1"] + b] = pair & t_high & ~high
    out[:, CI["lvl0"] + LEV] = t <= x
    out[:, CI["lvl1"] + LEV] = t >= x
    out[:, CI["msk0"] + LEV] = t == x
    out[:, CI["msk1"] + LEV] = t == x
    out[:, CI["pick"]] = (t % 32) == x
    return out


class Plan:

    def __init__(self):
        self.blocks = []
        self.stages = {}
        self.n_out = 0
        self.n_used = 0
        self.n_rows = 0

    def block(self, stage, cols, kc, outs_end):
        if outs_end is None:
            self.n_rows += 1
            release = ("rows", self.n_rows)
        elif outs_end:
            self.n_out += outs_end
            release = ("done", self.n_out)
        else:
            self.n_used += 1
            release = ("used", self.n_used)
        self.blocks.append((cols, kc, release))
        return len(self.blocks) - 1

    def stage(self, name, pieces):
        groups = []
        for parts, outs in pieces:
            first = self.n_out
            ids = [self.block(name, cols, kc, outs if i == len(parts) - 1 else 0)
                   for i, (cols, kc) in enumerate(parts)]
            groups.append((ids, first))
        self.stages[name] = groups


def make_plan():
    p = Plan()

    def layer_tail(i):
        p.stage(f"out{i}", [([(CB, KC), (CB, KC)], 2)] * (D // CB))
        p.stage(f"ff{i}", [([(CB, KC)], 2)] * (2 * D_FF // CB))
        p.stage(f"dn{i}", [([(CB, KC), (CB, KC), (CB, FC - 2 * KC)], 2)] * (D // CB))

    p.stage("mod0", [([(2 * CB, KC // 2)] * 2, 1)] * 12)
    p.stage("xbc", [([(CB, KC)], 2)] * (XBC_T // 2))
    p.stage("small0", [([(64, KC)], 2)])
    p.stage("z0", [([(CB, KC)], 2)] * 4)
    p.stage("qk0", [([(CB, KC)], 2)] * 4)
    p.stage("v0", [([(CB, KC)], 2)] * 4)
    p.stage("r0", [([(CB, KC)], 2)] * 4)
    p.stage("mod1", [([(2 * CB, KC // 2)] * 2, None)] * 12)
    layer_tail(0)
    p.stage("small1", [([(64, KC)], 1)])
    p.stage("qkv", [([(CB, KC)], 2)] * 16)
    p.stage("z1", [([(CB, KC)], 1)] * 8)
    layer_tail(1)
    return p


def pack_weights(w):
    slots = []

    def put(mat, r0, kc, c0, cols):
        a = np.zeros((P, KC * CB), mat.dtype)
        part = mat[r0:r0 + kc * P, c0:c0 + cols].reshape(kc, P, cols).transpose(1, 0, 2)
        a[:, :kc * cols] = part.reshape(P, kc * cols)
        slots.append(a)

    def wide(mat, c0, n, kcs=(KC,)):
        for j in range(n):
            r = 0
            for kc in kcs:
                put(mat, r * P, kc, c0 + j * CB, CB)
                r += kc

    def mod(i):
        for j in range(12):
            for half in range(2):
                put(w["mod_w"][i], half * D // 2, KC // 2, j * 2 * CB, 2 * CB)

    def tail(i, w_out):
        wide(w_out, 0, D // CB, (KC, KC))
        for j in range(D_FF // CB):
            put(w["ffn_w1"][i], 0, KC, j * CB, CB)
            put(w["ffn_w3"][i], 0, KC, j * CB, CB)
        wide(w["ffn_w2"][i], 0, D // CB, (KC, KC, FC - 2 * KC))

    ev, od = w["ev_w_in"][0], w["od_w_in"][0]
    mod(0)
    wide(ev, EV["xbc"], XBC_T // 2)
    put(np.concatenate([ev[:, EV["dt"]:EV["dt"] + 32], ev[:, EV["gl"]:EV["gl"] + 32]], 1), 0, KC, 0, 64)
    wide(ev, EV["z"], 4)
    wide(ev, EV["q"], 4)
    wide(ev, EV["v"], 4)
    wide(ev, EV["r"], 4)
    mod(1)
    tail(0, w["ev_w_out"][0])
    put(od, 0, KC, OD["ab"], 64)
    wide(od, OD["q"], 16)
    wide(od, OD["z"], 8)
    tail(1, w["od_w_out"][0])
    return np.stack(slots)


def pack_columns(w):
    def col(a):
        return np.ascontiguousarray(a).reshape(-1, P).T

    def conv(a):
        return a.reshape(TAPS, -1, P).transpose(2, 1, 0).reshape(P, -1)

    c2 = np.stack([w["c_ctx"], w["c"][0]]).reshape(2, KC, P).transpose(2, 1, 0).reshape(P, -1)
    parts = {"c": c2, "norm_mix": col(w["norm_mix"]), "norm_ffn": col(w["norm_ffn"]),
             "final": col(w["final_norm"]), "mod_b": col(w["mod_b"]),
             "conv_w0": conv(w["ssd_conv_w"][0]), "conv_b0": col(w["ssd_conv_b"][0]),
             "conv_w1": conv(w["gdn_conv_w"][0]), "ssd_norm": col(w["ssd_norm"][0]),
             "gla_norm": col(w["gla_norm"][0]), "gdn_norm": col(w["gdn_norm"][0])}
    return np.concatenate([parts[n] for n in COLS], 1)


def pack_rows(w):
    return np.concatenate([w["ssd_dt_bias"].reshape(-1), w["ssd_a_log"].reshape(-1), w["ssd_d"].reshape(-1),
                           w["gdn_dt_bias"].reshape(-1), w["gdn_a_log"].reshape(-1)])[None]


def pack_gate(w):
    g = np.zeros((2 * RANK + 1, 2, GLA_H * GLA_DK), w["gla_gate_w"].dtype)
    for d in DIRS:
        g[d * RANK:(d + 1) * RANK, d] = w["gla_gate_w"][0, d]
        g[2 * RANK, d] = w["gla_gate_b"][0, d]
    return g.reshape(2 * RANK + 1, -1)


def backbone(nc, x_in, w_in, cols_in, rows_in, gate_in, const_in, out):
    plan = make_plan()
    ctx = ExitStack()
    with ctx:
        def sb(name, shape):
            name += "_sb"
            return ctx.enter_context(nc.sbuf_tensor(name, shape, F32))

        def sem(name):
            return ctx.enter_context(nc.semaphore(name))

        xT = sb("xT", [P, KC, T])
        hT = sb("hT", [P, KC, T])
        ring = sb("ring", [P, RING, KC * CB])
        const = sb("const", [P, NCONST, P])
        cols = sb("cols", [P, NCOL])
        rows = sb("rows", [1, NROW])
        mod = sb("mod", [P, 2, 48, 2])
        gain = sb("gain", [P, 2, 2, KC, 2])
        wide = sb("wide", [P, 3, T])
        small = sb("small", [P, 1024])
        glT = sb("glT", [2 * RANK + 1, T])
        eps_col = sb("eps_col", [P, 2])
        ws = sb("ws", [P, 9216])
        arena = sb("arena", [P, 20480])
        psum = ctx.enter_context(nc.psum_tensor("psum", [P, 8, 512], F32))

        def cm(name, i=0):
            return const[:, CI[name] + i, :]

        def cms(name, n):
            return const[:, CI[name]:CI[name] + n, :]

        def cl(name, i=0, n=1):
            return cols[:, COLS[name][0] + i:COLS[name][0] + i + n]

        def area(where, start, *dims):
            n = int(np.prod(dims))
            a = where[:, start:start + n]
            assert start + n <= where.shape[1], (start, dims)
            names = "abcd"[:len(dims)]
            if len(dims) == 1:
                return a
            kw = {names[i]: dims[i] for i in range(len(dims) - 1)}
            return a.rearrange(f"p ({' '.join(names)}) -> p {' '.join(names)}", **kw)

        ident, ones, le, ge, gt, lt = (cm(n) for n in ("ident", "ones", "le", "ge", "gt", "lt"))
        upto_incl = (le, ge)
        beyond = (gt, lt)

        row_bc = small[:, 0:NROW]
        csilu = area(small, 144, KC, 2)
        a_exp = small[:, 160:224]
        stat = small[:, 224:256]
        edge = area(small, 256, TT, 96)
        dt = area(small, 640, TT, 32)
        da = area(small, 768, TT, 32)
        tmp128 = area(small, 896, TT, 32)

        beta, beta_up = dt, tmp128
        small_ab = area(ws, 4096, TT, 64)
        rs_q = area(ws, 0, QK_H, LAT)
        rs_k = area(ws, QK_H * LAT, QK_H, T)

        raw = area(ws, 0, 2, 2, CTX + 2 * PAD)
        conv = area(ws, 1040, 2, T)
        conv_out = area(ws, 2064, 2, T)

        mod_row = area(arena, 0, 6 * D)
        hidden = area(arena, 0, FC, T)
        gate_act = area(ws, 0, 4, T)
        mixT = area(arena, 0, 16, T)
        z0 = area(arena, 4096, TT, D)
        x0 = area(arena, 8192, TT, D)
        y0 = area(arena, 12288, TT, D)
        bT = area(arena, 16384, SSD_G, T)
        cT = area(arena, 17408, SSD_G, T)
        b_tok = area(arena, 18432, TT, SSD_G * P)
        g_mask = area(ws, 0, 2, SSD_G, TT, P)
        g_decay = area(ws, 2048, 2, 4, P)
        e_seg = area(ws, 3072, 2, 4, P)
        p_seg = area(ws, 4096, 2, 4, P)
        xdt = area(ws, 5120, SSD_H, SSD_P)
        xw = area(ws, 6144, SSD_H, SSD_P)
        ytmp = area(ws, 7168, 512)
        st0 = area(ws, 8192, SSD_G, 512)
        q0 = area(arena, 4096, GLA_H, T)
        k0 = area(arena, 6144, GLA_H, T)
        v0 = area(arena, 8192, TT, D)
        r0 = area(arena, 12288, TT, D)
        gk = area(arena, 16384, TT, 2, 512)
        o0 = hT[:, :, :].rearrange("p a b -> p (a b)").rearrange("p (a b) -> p a b", a=TT)
        el = area(ws, 0, 2, 8, P)
        qk = area(ws, 2048, 2, LEV, P)
        q_in = area(ws, 3840, 3, P)
        att0 = area(ws, 4224, 2, P)
        kdec0 = area(ws, 4480, 2, 512)
        st_gla = area(ws, 5504, GLA_H, GLA_DV)
        k_tok0 = area(ws, 6528, TT, 512)
        mod_piece = area(ws, 8576, 512)
        am = wide[:, 0:2, :].rearrange("p a (b c) -> p (a b) c", c=P)
        tile_decay = stat[:, 16:19]
        gtmp = area(ws, 0, 1024)
        gate = ws[0:2 * RANK + 1, 1024:2048]
        q1 = const[:, CI["lvl0"]:CI["lvl0"] + 16, :].rearrange("p a b -> p (a b)").rearrange("p (h t) -> p h t", h=QK_H)
        k1 = area(arena, 0, QK_H, T)
        k_tok1 = area(arena, 4096, TT, D)
        v1 = area(arena, 8192, TT, 2 * D)
        z1 = area(arena, 16384, 2, 2 * D)
        o1 = hT[:, :, :].rearrange("p a b -> p (a b)").rearrange("p (a b) -> p a b", a=2)
        mixT1 = area(arena, 0, 16, LAT)

        class GdnSet:

            def __init__(self, s):
                def buf(i):
                    return area(ws, (9 * s + i) * 512, 4, P)

                def by_dir(i):
                    return area(ws, (9 * s + i) * 512, 2, 2, P)
                self.first_bank = 4 * s
                self.decay, self.w = by_dir(0), buf(0)
                self.ea, self.vb = by_dir(1), buf(1)
                self.att = by_dir(2)
                self.a, self.vn = by_dir(3), buf(3)
                self.level, self.kd = by_dir(4), buf(4)
                self.x, self.nw = buf(5), buf(5)
                self.y, self.kb, self.s = buf(6), buf(7), buf(8)

            def signals(self, sems):
                (self.s_a, self.s_att, self.s_decay, self.s_dx, self.s_dy, self.s_ea, self.s_end, self.s_et, self.s_inv, self.s_kb, self.s_kd, self.s_level, self.s_new, self.s_nw, self.s_out, self.s_raw, self.s_seg, self.s_vn, self.s_w, self.s_wcopy, self.s_wt) = (sems[n] for n in sorted(sems))

            def flat(self, i):
                return psum[:, self.first_bank + i, :]

            def bank(self, i):
                return self.flat(i).rearrange("p (a b) -> p a b", a=4)

        gset = [GdnSet(0), GdnSet(1)]

        def tile(d, k):
            return slice(TILE_AT[d][k] * P, (TILE_AT[d][k] + 1) * P)

        def latent_tile(d, k):
            return slice((TILE_AT[d][k] - 2) * P, (TILE_AT[d][k] - 1) * P)

        s_in = sem("inputs_loaded")
        s_w = [sem(f"weights_ready{i}") for i in range(RING)]
        s_used = sem("weights_used")
        s_done = sem("gemm_done")
        s_drained = [sem(f"bank_drained{i}") for i in range(4)]
        s_out = sem("stored")
        s_gate = sem("gate_loaded")
        steps = {e: sem(f"{e}_step") for e in ("act", "dve", "pool")}
        S = {n: sem(n) for n in """
            ab_ln ab_raw beta_up c_ready decay dt_ln dt_raw edge edge_sums eps_set final_ready gk
            gk_ln gk_raw gl_ready gla_att gla_exp gla_karg gla_kdec gla_kexp gla_lv gla_masked gla_out
            gla_qk gla_scores gla_taken h_ready hidden k_copied k_tok k_tok1 k_tr k_tr1 l2_ln l2_mul l2_rs
            l2_sq l2_sum merged mix_rs mix_transposed mixed banks_zeroed mod_columns mod_copied mod_rows mod_taken residual rows_copied rows_spread rs scaled
            square square_used ssd_bc ssd_diag ssd_exp ssd_masked ssd_p ssd_pair ssd_r ssd_seg ssd_x ssd_y
            summed
            """.split()}
        conv_sems = {stage: {n: sem(f"{n}_{stage}") for n in "conv padded silu tr tr_taken".split()}
                     for stage in ("xbc", "qkv")}
        for s, G in enumerate(gset):
            G.signals({n: sem(f"gdn{s}_{n}") for n in
                       "a att decay dx dy ea end et inv kb kd level new nw out raw seg vn w wcopy wt".split()})
        block = ctx.enter_context(nc.Block())
        def drained(eng, b):
            eng.wait_ge(s_drained[b % 4], b // 4 + 1)

        def in_order(eng, steps):
            counts = {}

            def own(ins, s):
                counts[id(s)] = counts.get(id(s), 0) + 1
                eng.wait_ge(s, counts[id(s)])

            def link(ins):
                own(ins.then_inc(steps, 1), steps)
            return link, own

        def out_of(stage, g, f=0):
            return plan.stages[stage][g][1] + f

        CONVS = {"xbc": dict(tiles=XBC_T, n_tr=10, q_tiles=0, w="conv_w0"),
                 "qkv": dict(tiles=32, n_tr=32, q_tiles=8, w="conv_w1")}

        def conv_dest(stage, t):
            if stage == "xbc":
                return None if t < 8 else bT[:, t - 8] if t < 10 else cT[:, t - 10]
            return q1[:, t] if t < 8 else k1[:, t - 8] if t < 16 else None

        def transposed(stage, t):
            if stage == "xbc":
                return t if t < 10 else None
            return t - 16 if t >= 16 else None

        def segs(stage, t):
            return (1,) if t < CONVS[stage]["q_tiles"] else (0, 1)

        def seg(s):
            return slice(s * CTX, s * CTX + LAT)

        def span(stage, t):
            return slice(segs(stage, t)[0] * CTX, T)

        NORM_AT = {"mix0": (0, 0), "ffn0": (1, 16), "mix1": (2, 32), "ffn1": (3, 48), "fin": (4, 56)}
        MIX_AT = {"ssd": (0, 0), "gla": (8, 1), "gdn": (16, 2)}
        NORMS = {"mix0": (0, 0, 0), "ffn0": (0, 1, 0), "mix1": (1, 0, 0), "ffn1": (1, 1, 1), "fin": (None, None, 1)}

        @block.sync
        def _(sp):
            sp.dma_start(const[:, :, :], const_in.rearrange("p (a b) -> p a b", b=P)).then_inc(s_in, 16)
            sp.dma_start(cols[:, :], cols_in).then_inc(s_in, 16)
            sp.dma_start(rows[:, :], rows_in).then_inc(s_in, 16)
            sp.dma_start(xT[:, :, :], x_in.rearrange("p (a b) -> p a b", b=T)).then_inc(s_in, 16)
            for n, (ncol, kc, release) in enumerate(plan.blocks):
                if n >= RING:
                    kind, value = plan.blocks[n - RING][2]
                    sp.wait_ge({"done": s_done, "used": s_used, "rows": S["mod_rows"]}[kind], value)
                sp.dma_start(ring[:, n % RING, 0:kc * ncol], w_in[n, :, 0:kc * ncol]).then_inc(s_w[n % RING], 16)
            sp.wait_ge(S["final_ready"], KC)
            sp.dma_start(out.rearrange("p (a b) -> p a b", b=LAT), xT[:, :, CTX:T]).then_inc(s_out, 16)
            sp.wait_ge(s_out, 16)

        @block.tensor
        def _(pe):
            def mm(o, l, r, start=True, stop=True):
                return nc.tensor.matmul(o, l, r, start=start, stop=stop)

            def slot(n, ncol, kc):
                return ring[:, n % RING, 0:kc * ncol].rearrange("p (c n) -> p c n", c=kc)

            def block_ready(n):
                pe.wait_ge(s_w[n % RING], 16 * (n // RING + 1))

            def bank_free(b):
                if b >= 4:
                    pe.wait_ge(s_drained[b % 4], b // 4)

            def chunk_ready(tag, c):
                n = 2 - NORMS[tag][2]
                pe.wait_ge(S["h_ready"], NORM_AT[tag][1] + (c + 1) * n)

            def gemm(stage, g, src, total, lo=0, after=None):
                ids, first = plan.stages[stage][g]
                at = 0
                for i, n in enumerate(ids):
                    ncol, kc, _ = plan.blocks[n]
                    w = slot(n, ncol, kc)
                    block_ready(n)
                    for f in range(2):
                        b = first + f
                        if i == 0:
                            bank_free(b)
                        for c in range(kc):
                            if after and f == 0:
                                chunk_ready(after, c)
                            last = mm(psum[:, b % 4, lo:T], w[:, c, f * P:(f + 1) * P], src(at + c),
                                      start=(at + c == 0), stop=(at + c == total - 1))
                        if i == len(ids) - 1:
                            last.then_inc(s_done, 1)
                    if i < len(ids) - 1:
                        last.then_inc(s_used, 1)
                    at += kc

            def gemm_tok(stage, g, tiles):
                ids, first = plan.stages[stage][g]
                w = slot(ids[0], CB, KC)
                block_ready(ids[0])
                for f in range(len(tiles) // 2):
                    bank_free(first + f)
                    for jj in range(2):
                        for c in range(KC):
                            last = mm(psum[:, (first + f) % 4, jj * CB:(jj + 1) * CB],
                                      hT[:, c, tiles[2 * f + jj] * P:(tiles[2 * f + jj] + 1) * P], w[:, c, :],
                                      start=(c == 0), stop=(c == KC - 1))
                    last.then_inc(s_done, 1)

            def mod_products(ids, bank):
                for half, n in enumerate(ids):
                    w = slot(n, 2 * CB, KC // 2)
                    block_ready(n)
                    for c in range(KC // 2):
                        last = mm(psum[32 * c:32 * c + 2, bank, :], csilu[:, half * KC // 2 + c, :], w[:, c, :],
                                  start=(half == 0), stop=(half == 1))
                    if half == 0:
                        last.then_inc(s_used, 1)
                return last

            def modulation0():
                pe.wait_ge(S["banks_zeroed"], 1)
                for q in range(12):
                    ids, b = plan.stages["mod0"][q]
                    bank_free(b)
                    mod_products(ids, b % 4).then_inc(s_done, 1)
                for q in range(12):
                    drained(pe, out_of("mod0", q))
                    for t in range(4 * q, 4 * q + 4):
                        last = mm(psum[:, 4, 2 * t:2 * t + 2], mod_row[:, t * P:(t + 1) * P], cm("pick")[:, 0:2])
                last.then_inc(S["mod_columns"], 1)

            def mod1_rows(q):
                if q > 0:
                    pe.wait_ge(S["mod_taken"], q)
                mod_products(plan.stages["mod1"][q][0], 3).then_inc(S["mod_rows"], 1)

            def mod1_columns(q):
                pe.wait_ge(S["mod_copied"], q + 1)
                for t in range(4):
                    last = mm(psum[:, 3, 2 * t:2 * t + 2], mod_piece[:, t * P:(t + 1) * P], cm("pick")[:, 0:2])
                last.then_inc(S["mod_columns"], 1)

            def norm_sum(tag, c):
                lo = NORMS[tag][2] * CTX
                pe.wait_ge(S["square"], NORM_AT[tag][0] * KC + c + 1)
                mm(psum[:, 5, lo:T], ones, wide[:, c % 2, lo:T], start=(c == 0), stop=(c == KC - 1)).then_inc(S["square_used"], 1)

            def gemm_and_norm(stage, src, total, tag):
                for g in range(D // CB):
                    gemm(stage, g, src, total, lo=NORMS[tag][2] * CTX)
                    for c in (2 * g - 2, 2 * g - 1):
                        if c >= 0:
                            norm_sum(tag, c)
                norm_sum(tag, KC - 2)
                norm_sum(tag, KC - 1)

            def conv_stage(stage):
                C = conv_sems[stage]
                info = CONVS[stage]
                for g in range(info["tiles"] // 2):
                    gemm(stage, g, lambda c, s=span(stage, 2 * g): hT[:, c, s], KC, lo=span(stage, 2 * g).start,
                         after="mix0" if stage == "xbc" and g == 0 else None)
                    for t in (2 * g - 2, 2 * g - 1):
                        if t >= 0:
                            transpose_conv(stage, t)
                for t in (info["tiles"] - 2, info["tiles"] - 1):
                    transpose_conv(stage, t)

            def transpose_conv(stage, t):
                C = conv_sems[stage]
                n = transposed(stage, t)
                if n is None:
                    return
                dest = conv_dest(stage, t)
                src = dest if dest is not None else conv_out[:, n % 2]
                pe.wait_ge(C["silu"], t + 1)
                if n - 1 > 0:
                    pe.wait_ge(C["tr_taken"], n - 1)
                for j in range(TT):
                    last = nc.tensor.transpose(psum[:, 6 + n % 2, j * P:(j + 1) * P], src[:, j * P:(j + 1) * P], ident)
                last.then_inc(C["tr"], 1)

            def small0():
                ids, b = plan.stages["small0"][0]
                w = slot(ids[0], 64, KC)
                block_ready(ids[0])
                bank_free(b)
                for j in range(TT):
                    for c in range(KC):
                        last = mm(psum[:, b % 4, j * 32:(j + 1) * 32], hT[:, c, j * P:(j + 1) * P], w[:, c, 0:32],
                                  start=(c == 0), stop=(c == KC - 1))
                last.then_inc(s_done, 1)
                bank_free(b + 1)
                for c in range(KC):
                    last = mm(psum[0:32, (b + 1) % 4, :], w[:, c, 32:64], hT[:, c, :], start=(c == 0), stop=(c == KC - 1))
                last.then_inc(s_done, 1)

            def small1():
                ids, b = plan.stages["small1"][0]
                w = slot(ids[0], 64, KC)
                block_ready(ids[0])
                bank_free(b)
                for j in range(TT):
                    for c in range(KC):
                        if j == 0:
                            chunk_ready("mix1", c)
                        last = mm(psum[:, b % 4, j * 64:(j + 1) * 64], hT[:, c, j * P:(j + 1) * P], w[:, c, :],
                                  start=(c == 0), stop=(c == KC - 1))
                last.then_inc(s_done, 1)

            def edges(layer):
                pe.wait_ge(S["decay"], layer + 1)
                for j in range(TT):
                    for d in DIRS:
                        mm(psum[:, 4, j * 96 + d * 16:j * 96 + d * 16 + 16], beyond[d], da[:, j, d * 16:d * 16 + 16])
                        mm(psum[:, 4, j * 96 + 32 + d * 16:j * 96 + 48 + d * 16], upto_incl[d], da[:, j, d * 16:d * 16 + 16])
                    last = mm(psum[:, 4, j * 96 + 64:j * 96 + 96], ones, da[:, j, :])
                last.then_inc(S["edge_sums"], 1)

            def ssd():
                edges(0)
                for g in range(SSD_G):
                    for j in range(TT):
                        last = mm(psum[:, 5 + g, j * P:(j + 1) * P], bT[:, g, j * P:(j + 1) * P], cT[:, g, j * P:(j + 1) * P])
                last.then_inc(S["ssd_bc"], 1)
                pe.wait_ge(S["ssd_masked"], 4)
                pe.wait_ge(S["edge"], 1)

                def decay(u):
                    pe.wait_ge(S["ssd_r"], u + 1)
                    if u - 1 > 0:
                        pe.wait_ge(S["ssd_exp"], u - 1)
                    mm(psum[:, 4 + u % 2, :], beyond[u // 16], g_decay[:, u % 2].rearrange("p a b -> p (a b)")).then_inc(S["ssd_seg"], 1)

                decay(0)
                for u in range(32):
                    if u + 1 < 32:
                        decay(u + 1)
                    d, k, g, hq = u // 16, u // 4 % 4, u // 2 % 2, u % 2
                    j = TILE_AT[d][k]
                    v = u // 2
                    pe.wait_ge(S["ssd_p"], u + 1)
                    if hq == 0:
                        if v - 1 > 0:
                            pe.wait_ge(S["ssd_y"], v - 1)
                        pe.wait_ge(S["ssd_x"], u // 4 + 1)
                    for i in range(4):
                        h = hq * 4 + i
                        last = mm(psum[:, 6 + v % 2, h * 64:(h + 1) * 64], p_seg[:, u % 2, i], xdt[:, g * 8 + h])
                    last.then_inc(S["ssd_diag"], 1)
                    if hq == 1:
                        if k > 0:
                            mm(psum[:, 2 + v % 2, :], cT[:, g, j * P:(j + 1) * P], st0[:, g])
                        last = mm(psum[:, v % 2, :], b_tok[:, j, g * P:(g + 1) * P],
                                  xw[:, g * 8:(g + 1) * 8].rearrange("p a b -> p (a b)"))
                        last.then_inc(S["ssd_pair"], 1)

            def transpose_mix(tag, src, n_tiles, toks):
                pe.wait_ge(S["merged"], MIX_AT[tag][1] + 1)
                for t in range(n_tiles):
                    if MIX_AT[tag][0] + t - 1 > 0:
                        pe.wait_ge(S["mixed"], MIX_AT[tag][0] + t - 1)
                    for j in range(toks):
                        last = nc.tensor.transpose(psum[:, 6 + t % 2, j * P:(j + 1) * P], src[:, j, t * P:(t + 1) * P], ident)
                    last.then_inc(S["mix_transposed"], 1)

            def gla():
                pe.wait_ge(S["gl_ready"], 1)
                for j in range(TT):
                    if j > 0:
                        pe.wait_ge(S["gk"], j)
                    for d in DIRS:
                        last = mm(psum[:, 4 + d, :], glT[:, j * P:(j + 1) * P], gate[:, d * 512:(d + 1) * 512])
                    last.then_inc(S["gk_raw"], 1)
                pe.wait_ge(S["k_copied"], 1)
                for h in range(GLA_H):
                    if h - 1 > 0:
                        pe.wait_ge(S["k_tok"], h - 1)
                    for j in range(TT):
                        last = nc.tensor.transpose(psum[:, 6 + h % 2, j * P:(j + 1) * P], k0[:, h, j * P:(j + 1) * P], ident)
                    last.then_inc(S["k_tr"], 1)
                pe.wait_ge(S["gk"], TT)
                pe.wait_ge(S["k_tok"], GLA_H)

                def levels(w):
                    d, k, h = w // 16, w // 4 % 4, w % 4
                    j = TILE_AT[d][k]
                    if h == 0:
                        if w // 4 > 0:
                            pe.wait_ge(S["gla_kexp"], w // 4)
                        mm(psum[:, 0, :], beyond[d], gk[:, j, d]).then_inc(S["gla_karg"], 1)
                    if w > 0:
                        pe.wait_ge(S["gla_exp"], w)
                    c = cms(f"lvl{d}", 8)
                    for i in range(2):
                        last = mm(psum[:, 4 + i, :], gk[:, j, d, h * P:(h + 1) * P],
                                  c[:, 4 * i:4 * i + 4, :].rearrange("p a b -> p (a b)"))
                    last.then_inc(S["gla_lv"], 1)

                def scores(w):
                    d, k, h = w // 16, w // 4 % 4, w % 4
                    j = TILE_AT[d][k]
                    pe.wait_ge(S["gla_qk"], w + 1)
                    if w > 0:
                        pe.wait_ge(S["gla_masked"], w)
                    for b in range(LEV):
                        mm(psum[:, 6 + b // 4, b % 4 * P:(b % 4 + 1) * P], qk[:, w % 2, b], qk[:, w % 2, b])
                    mm(psum[:, 7, 3 * P:4 * P], k0[:, h, j * P:(j + 1) * P], q0[:, h, j * P:(j + 1) * P]).then_inc(S["gla_scores"], 1)

                def outputs(w):
                    d, k, h = w // 16, w // 4 % 4, w % 4
                    j = TILE_AT[d][k]
                    pe.wait_ge(S["gla_att"], w + 1)
                    if w > 0:
                        pe.wait_ge(S["gla_taken"], w)
                    vh = v0[:, j, h * GLA_DV:(h + 1) * GLA_DV]
                    mm(psum[:, 1, 0:GLA_DV], att0[:, w % 2], vh, stop=(k == 0))
                    if k > 0:
                        mm(psum[:, 1, 0:GLA_DV], q_in[:, w % 3], st_gla[:, h], start=False)
                    pe.wait_ge(S["gla_kdec"], w // 4 + 1)
                    mm(psum[:, 2, 0:GLA_DV], kdec0[:, w // 4 % 2, h * P:(h + 1) * P], vh).then_inc(S["gla_out"], 1)

                levels(0)
                levels(1)
                for w in range(32):
                    scores(w)
                    if w > 0:
                        outputs(w - 1)
                    if w + 2 < 32:
                        levels(w + 2)
                    if w < 24 and w % 2 == 0:
                        mod1_rows(w // 2)
                    elif w < 24:
                        mod1_columns(w // 2)
                outputs(31)

            def l2():
                for t in range(16):
                    lo = CTX if t < 8 else 0
                    pe.wait_ge(S["l2_sq"], t + 1)
                    if t - 1 > 0:
                        pe.wait_ge(S["l2_ln"], t - 1)
                    mm(psum[:, 4 + t % 2, lo:T], ones, wide[:, t % 2, lo:T]).then_inc(S["l2_sum"], 1)
                for h in range(QK_H):
                    pe.wait_ge(S["l2_mul"], 8 + h + 1)
                    if h - 1 > 0:
                        pe.wait_ge(S["k_tok1"], h - 1)
                    for j in range(TT):
                        last = nc.tensor.transpose(psum[:, 6 + h % 2, j * P:(j + 1) * P], k1[:, h, j * P:(j + 1) * P], ident)
                    last.then_inc(S["k_tr1"], 1)
                pe.wait_ge(S["k_tok1"], QK_H)

            def ffn(i):
                lo = i * CTX
                for j in range(2 * D_FF // CB):
                    gemm(f"ff{i}", j, lambda c: hT[:, c, lo:T], KC, lo=lo, after=f"ffn{i}" if j == 0 else None)
                pe.wait_ge(S["hidden"], (i + 1) * FC)
                gemm_and_norm(f"dn{i}", lambda c: hidden[:, c, lo:T], FC, ("mix1", "fin")[i])

            def gdn():
                def seg_products(n, s):
                    G, hq, k = gset[s], 2 * (n // 4) + s, n % 4
                    pe.wait_ge(G.s_decay, n + 1)
                    if n > 0:
                        pe.wait_ge(G.s_end, n)
                    for d in DIRS:
                        tok = tile(d, k)
                        mm(G.bank(2)[:, d], k1[:, hq, tok], k1[:, hq, tok])
                        if k >= 2:
                            mm(G.bank(2)[:, 2 + d], k1[:, hq, tok], q1[:, hq, latent_tile(d, k)])
                    for d in DIRS:
                        for v in range(2):
                            last = mm(G.bank(0)[:, 2 * d + v], G.decay[:, d, v], beyond[d])
                        if k >= 2:
                            last = mm(G.flat(1)[:, d * 256:(d + 1) * 256], beyond[d],
                                      G.decay[:, d].rearrange("p a b -> p (a b)"))
                    last.then_inc(G.s_seg, 1)

                def first_inverse(n, s):
                    G = gset[s]
                    pe.wait_ge(G.s_level, 7 * n + 1)
                    for m in range(4):
                        last = mm(G.bank(0)[:, m], G.level[:, m // 2, m % 2], ident)
                    last.then_inc(G.s_w, 1)

                def level_w(n, s, b):
                    G = gset[s]
                    pe.wait_ge(G.s_inv, 7 * n + b)
                    pe.wait_ge(G.s_level, 7 * n + b + 1)
                    for m in range(4):
                        last = mm(G.bank(2)[:, m], G.level[:, m // 2, m % 2], G.y[:, m])
                    last.then_inc(G.s_w, 1)

                def level_d(n, s, b):
                    G = gset[s]
                    pe.wait_ge(G.s_wcopy, 6 * n + b)
                    for m in range(4):
                        last = mm(G.bank(0)[:, m], G.x[:, m], G.w[:, m])
                    last.then_inc(G.s_dy, 1)
                    if b < LEV - 1:
                        for m in range(4):
                            last = mm(G.bank(1)[:, m], G.w[:, m], G.x[:, m])
                        last.then_inc(G.s_dx, 1)

                def state_reads(n, s):
                    G, k = gset[s], n % 4
                    if k == 0:
                        return
                    pe.wait_ge(G.s_inv, 7 * n + 7)
                    pe.wait_ge(G.s_kb, n + 1)
                    for m in range(4):
                        last = mm(G.bank(2)[:, m], G.kb[:, m], G.y[:, m])
                    last.then_inc(G.s_wt, 1)

                def new_values(n, s):
                    G, hq, k = gset[s], 2 * (n // 4) + s, n % 4
                    pe.wait_ge(G.s_inv, 7 * n + 7)
                    pe.wait_ge(G.s_kb, n + 1)
                    if k > 0:
                        pe.wait_ge(G.s_nw, n // 4 * 3 + k)
                    for m in range(4):
                        last = mm(G.bank(3)[:, m], G.y[:, m], G.vb[:, m], stop=(k == 0))
                        if k > 0:
                            last = mm(G.bank(3)[:, m], G.nw[:, m], G.s[:, m], start=False)
                    if k >= 2:
                        for d in DIRS:
                            last = mm(G.flat(0)[:, d * 256:(d + 1) * 256], q1[:, hq, latent_tile(d, k)],
                                      G.s[:, 2 * d:2 * d + 2].rearrange("p a b -> p (a b)"))
                    last.then_inc(G.s_new, 1)

                def outputs(n, s):
                    G, k = gset[s], n % 4
                    pe.wait_ge(G.s_vn, n + 1)
                    if k >= 2:
                        pe.wait_ge(G.s_att, n // 4 * 2 + k - 1)
                        for m in range(4):
                            last = mm(G.bank(1)[:, m], G.att[:, m // 2, m % 2], G.vn[:, m])
                    if k < 3:
                        pe.wait_ge(G.s_kd, n + 1)
                        for m in range(4):
                            last = mm(G.bank(2)[:, m], G.kd[:, m], G.vn[:, m])
                    last.then_inc(G.s_out, 1)

                for n in range(16):
                    for s in range(2):
                        seg_products(n, s)
                    for s in range(2):
                        first_inverse(n, s)
                    for b in range(1, LEV):
                        for s in range(2):
                            level_w(n, s, b)
                        for s in range(2):
                            level_d(n, s, b)
                    for s in range(2):
                        state_reads(n, s)
                    for s in range(2):
                        new_values(n, s)
                    for s in range(2):
                        outputs(n, s)

            pe.wait_ge(s_in, 64)
            mm(psum[:, 7, 0:NROW], ones[0:1, :], rows[0:1, :]).then_inc(S["rows_spread"], 1)
            pe.wait_ge(S["c_ready"], 1)
            modulation0()
            for c in range(KC):
                norm_sum("mix0", c)
            conv_stage("xbc")
            small0()
            for g in range(4):
                gemm_tok("z0", g, (0, 1, 2, 3))
            ssd()
            transpose_mix("ssd", y0, 8, TT)
            pe.wait_ge(S["mixed"], 8)
            for g in range(4):
                gemm("qk0", g, lambda c: hT[:, c, :], KC)
            for stage in ("v0", "r0"):
                for g in range(4):
                    gemm_tok(stage, g, (0, 1, 2, 3))
            pe.wait_ge(s_gate, 16)
            gla()
            transpose_mix("gla", o0, 8, TT)
            pe.wait_ge(S["mixed"], 16)
            gemm_and_norm("out0", lambda c: mixT[:, c, :], 16, "ffn0")
            ffn(0)
            small1()
            conv_stage("qkv")
            for g in range(8):
                gemm_tok("z1", g, (2, 3))
            l2()
            edges(1)
            pe.wait_ge(S["edge"], 2)
            gdn()
            transpose_mix("gdn", o1, 16, 2)
            pe.wait_ge(S["mixed"], 32)
            gemm_and_norm("out1", lambda c: mixT1[:, c, :], 16, "ffn1")
            ffn(1)

        @block.scalar
        def _(act):
            link, own = in_order(act, steps["act"])

            def f(o, i, func, **kw):
                return nc.scalar.activation(o, i, func, **kw)

            def modulation0():
                for q in range(12):
                    b = out_of("mod0", q)
                    act.wait_ge(s_done, b + 1)
                    f(mod_row[:, q * 512:(q + 1) * 512], psum[:, b % 4, :], ACT.Copy).then_inc(s_drained[b % 4], 1)
                    act.wait_ge(s_drained[b % 4], b // 4 + 1)

            def norm(tag):
                i, which, s_lo = NORMS[tag]
                lo = s_lo * CTX
                n, h_before = NORM_AT[tag]
                for c in range(KC):
                    if n > 0:
                        act.wait_ge(S["residual"], (n - 1) * KC + c + 1)
                    if n * KC + c - 1 > 0:
                        act.wait_ge(S["square_used"], n * KC + c - 1)
                    own(f(wide[:, c % 2, lo:T], xT[:, c, lo:T], ACT.Square).then_inc(S["square"], 1), S["square"])
                act.wait_ge(S["square_used"], (n + 1) * KC)
                link(f(wide[:, 2, lo:T], psum[:, 5, lo:T], ACT.Ln, scale=1.0 / D, bias=eps_col[:, 0:1]))
                own(f(wide[:, 2, lo:T], wide[:, 2, lo:T], ACT.Exp, scale=-0.5).then_inc(S["rs"], 1), S["rs"])
                if tag == "fin":
                    return
                for c in range(KC):
                    for s in range(s_lo, 2):
                        h = hT[:, c, seg(s)]
                        act.wait_ge(S["scaled"], h_before + c * (2 - s_lo) + s - s_lo + 1)
                        own(f(h, h, ACT.Identity, bias=mod[:, i, 24 * which + c, s:s + 1]).then_inc(S["h_ready"], 1), S["h_ready"])

            def conv_stage(stage):
                C = conv_sems[stage]
                n_tiles = CONVS[stage]["tiles"]

                def activate(t):
                    n = transposed(stage, t)
                    sl = span(stage, t)
                    dest = conv_dest(stage, t)
                    act.wait_ge(C["conv"], t + 1)
                    if dest is None:
                        if n - 1 > 0:
                            act.wait_ge(C["tr"], n - 1)
                        dest = conv_out[:, n % 2]
                    own(f(dest if stage == "qkv" and t < 8 else dest[:, sl], conv[:, t % 2, sl], ACT.Silu).then_inc(C["silu"], 1), C["silu"])

                for t in range(n_tiles):
                    b = out_of(stage, t // 2, t % 2)
                    if t > 1:
                        act.wait_ge(C["conv"], t - 1)
                    else:
                        act.wait_ge(C["padded"], 1)
                    s0, s1 = segs(stage, t)[0], segs(stage, t)[-1] + 1
                    act.wait_ge(s_done, b + 1)
                    f(raw[:, t % 2, s0:s1, PAD:PAD + CTX], psum[:, b % 4, s0 * CTX:T].rearrange("p (s t) -> p s t", t=CTX), ACT.Copy).then_inc(s_drained[b % 4], 1)
                    act.wait_ge(s_drained[b % 4], b // 4 + 1)
                    if t > 0:
                        activate(t - 1)
                activate(n_tiles - 1)

            def log1p_exp_neg_abs(o, i, s):
                link(f(o, i, ACT.Abs))
                link(f(o, o, ACT.Exp, scale=-1.0))
                own(f(o, o, ACT.Ln, bias=1.0).then_inc(s, 1), s)

            def edges(layer):
                act.wait_ge(S["edge_sums"], layer + 1)
                own(f(edge[:, :, :], psum[:, 4, 0:TT * 96].rearrange("p (a b) -> p a b", a=TT), ACT.Exp).then_inc(S["edge"], 1), S["edge"])

            def ssd():
                edges(0)
                for u in range(32):
                    act.wait_ge(S["ssd_seg"], u + 1)
                    if u - 1 > 0:
                        act.wait_ge(S["ssd_p"], u - 1)
                    own(f(e_seg[:, u % 2], psum[:, 4 + u % 2, :].rearrange("p (a b) -> p a b", a=4), ACT.Exp).then_inc(S["ssd_exp"], 1), S["ssd_exp"])
                act.wait_ge(S["summed"], 1)
                for j in range(TT):
                    for g in range(SSD_G):
                        link(f(ws[:, 0:512], y0[:, j, g * 512:(g + 1) * 512], ACT.Square, accum_out=stat[:, j * 2 + g:j * 2 + g + 1]))
                link(f(stat[:, 0:8], stat[:, 0:8], ACT.Ln, scale=1.0 / 512, bias=eps_col[:, 0:1]))
                own(f(stat[:, 0:8], stat[:, 0:8], ACT.Exp, scale=-0.5).then_inc(S["mix_rs"], 1), S["mix_rs"])
                mixed("ssd", 8, 0, lambda t: cl("ssd_norm", t), mixT, T)

            def mixed(tag, n_tiles, at, scale, dest, width):
                for t in range(n_tiles):
                    act.wait_ge(S["mix_transposed"], MIX_AT[tag][0] + t + 1)
                    own(f(dest[:, at + t, :], psum[:, 6 + t % 2, 0:width], ACT.Copy, scale=scale(t)).then_inc(S["mixed"], 1), S["mixed"])

            def gla():
                for t in range(8):
                    b = out_of("qk0", t // 2, t % 2)
                    act.wait_ge(s_done, b + 1)
                    f(q0[:, t] if t < 4 else k0[:, t - 4], psum[:, b % 4, :], ACT.Copy, scale=GLA_DK ** -0.5 if t < 4 else 1.0).then_inc(s_drained[b % 4], 1)
                    act.wait_ge(s_drained[b % 4], b // 4 + 1)
                own(f(stat[:, 0:1], stat[:, 0:1], ACT.Copy).then_inc(S["k_copied"], 1), S["k_copied"])
                for stage, dest, func in (("v0", v0, ACT.Copy), ("r0", r0, ACT.Silu)):
                    for g in range(4):
                        for i in range(2):
                            b = out_of(stage, g, i)
                            act.wait_ge(s_done, b + 1)
                            f(dest[:, 2 * i:2 * i + 2, g * CB:(g + 1) * CB], psum[:, b % 4, :].rearrange("p (a b) -> p a b", a=2), func).then_inc(s_drained[b % 4], 1)
                            act.wait_ge(s_drained[b % 4], b // 4 + 1)
                for j in range(TT):
                    act.wait_ge(S["gk_raw"], j + 1)
                    if j > 0:
                        act.wait_ge(S["gk"], j)
                    log1p_exp_neg_abs(gtmp.rearrange("p (a b) -> p a b", a=2), psum[:, 4:6, :], S["gk_ln"])
                for w in range(32):
                    act.wait_ge(S["gla_lv"], w + 1)
                    if w - 1 > 0:
                        act.wait_ge(S["gla_qk"], w - 1)
                    own(f(el[:, w % 2].rearrange("p a b -> p (a b)").rearrange("p (a b) -> p a b", a=2), psum[:, 4:6, :],
                          ACT.Exp, scale=1.0 / GLA_NORM).then_inc(S["gla_exp"], 1), S["gla_exp"])
                    if w % 4 == 0:
                        act.wait_ge(S["gla_karg"], w // 4 + 1)
                        if w > 4:
                            act.wait_ge(S["gla_out"], w - 4)
                        own(f(kdec0[:, w // 4 % 2], psum[:, 0, :], ACT.Exp, scale=1.0 / GLA_NORM).then_inc(S["gla_kexp"], 1), S["gla_kexp"])
                    if w % 2 == 0 and 0 < w <= 24:
                        q = w // 2 - 1
                        act.wait_ge(S["mod_rows"], q + 1)
                        own(f(mod_piece, psum[:, 3, :], ACT.Copy).then_inc(S["mod_copied"], 1), S["mod_copied"])
                act.wait_ge(S["summed"], 2)
                for j in range(TT):
                    for h in range(GLA_H):
                        link(f(ws[:, 0:GLA_DV], o0[:, j, h * GLA_DV:(h + 1) * GLA_DV], ACT.Square,
                          accum_out=stat[:, j * 4 + h:j * 4 + h + 1]))
                link(f(stat[:, 0:16], stat[:, 0:16], ACT.Ln, scale=1.0 / GLA_DV, bias=eps_col[:, 0:1]))
                own(f(stat[:, 0:16], stat[:, 0:16], ACT.Exp, scale=-0.5).then_inc(S["mix_rs"], 1), S["mix_rs"])
                mixed("gla", 8, 8, lambda t: cl("gla_norm", t % 2), mixT, T)

            def ffn(i):
                lo = i * CTX
                for g in range(D_FF // CB):
                    for ff in range(2):
                        t = 2 * g + ff
                        b = out_of(f"ff{i}", 2 * g, ff)
                        if i * FC + t - 3 > 0:
                            act.wait_ge(S["hidden"], i * FC + t - 3)
                        act.wait_ge(s_done, b + 1)
                        f(gate_act[:, t % 4, lo:T], psum[:, b % 4, lo:T], ACT.Silu).then_inc(s_drained[b % 4], 1)
                        act.wait_ge(s_drained[b % 4], b // 4 + 1)

            def gdn_inputs():
                act.wait_ge(S["ab_raw"], 1)
                link(f(dt, small_ab[:, :, 32:64], ACT.Sigmoid))
                log1p_exp_neg_abs(tmp128, small_ab[:, :, 0:32], S["ab_ln"])

            def z_and_l2():
                for g in range(8):
                    b = out_of("z1", g)
                    act.wait_ge(s_done, b + 1)
                    f(z1[:, :, g * CB:(g + 1) * CB], psum[:, b % 4, :].rearrange("p (a b) -> p a b", a=2), ACT.Silu).then_inc(s_drained[b % 4], 1)
                    act.wait_ge(s_drained[b % 4], b // 4 + 1)
                for t in range(16):
                    lo = CTX if t < 8 else 0
                    src = q1[:, t] if t < 8 else k1[:, t - 8]
                    if t - 1 > 0:
                        act.wait_ge(S["l2_sum"], t - 1)
                    own(f(wide[:, t % 2, lo:T], src, ACT.Square).then_inc(S["l2_sq"], 1), S["l2_sq"])
                    if t > 0:
                        log_norm(t - 1)
                log_norm(15)
                for t in range(16):
                    r = rs_q[:, t] if t < 8 else rs_k[:, t - 8]
                    own(f(r, r, ACT.Exp, scale=-0.5, bias=eps_col[:, 1:2] if t < 8 else 0.0).then_inc(S["l2_rs"], 1), S["l2_rs"])
                edges(1)

            def log_norm(t):
                lo = CTX if t < 8 else 0
                act.wait_ge(S["l2_sum"], t + 1)
                own(f(rs_q[:, t] if t < 8 else rs_k[:, t - 8], psum[:, 4 + t % 2, lo:T], ACT.Ln, bias=eps_col[:, 0:1]).then_inc(S["l2_ln"], 1), S["l2_ln"])

            def gdn():
                def exps(n, s):
                    G, k = gset[s], n % 4
                    act.wait_ge(G.s_seg, n + 1)
                    own(f(G.ea.rearrange("p a b c -> p (a b c)"), G.flat(0), ACT.Exp).then_inc(G.s_ea, 1), G.s_ea)
                    if k >= 2:
                        own(f(G.att.rearrange("p a b c -> p (a b c)"), G.flat(1), ACT.Exp).then_inc(G.s_et, 1), G.s_et)

                def wcopy(n, s, b):
                    G = gset[s]
                    act.wait_ge(G.s_w, 7 * n + b + 1)
                    own(f(G.w.rearrange("p a b -> p (a b)"), G.flat(2), ACT.Copy).then_inc(G.s_wcopy, 1), G.s_wcopy)

                def values(n, s):
                    G, hq, k = gset[s], 2 * (n // 4) + s, n % 4
                    act.wait_ge(G.s_a, n + 1)
                    for m in range(4):
                        d, v = m // 2, 2 * hq + m % 2
                        j = TILE_AT[d][k]
                        link(f(G.vb[:, m], v1[:, j, v * P:(v + 1) * P], ACT.Copy, scale=beta[:, j, d * 16 + v:d * 16 + v + 1]))
                        ins = f(G.kb[:, m], k_tok1[:, j, hq * P:(hq + 1) * P], ACT.Copy, scale=beta_up[:, j, d * 16 + v:d * 16 + v + 1])
                        if m == 3:
                            own(ins.then_inc(G.s_kb, 1), G.s_kb)
                        else:
                            link(ins)

                def kdecay(n, s):
                    G, hq, k = gset[s], 2 * (n // 4) + s, n % 4
                    act.wait_ge(G.s_w, 7 * n + 7)
                    for m in range(4):
                        d, v = m // 2, 2 * hq + m % 2
                        j = TILE_AT[d][k]
                        ins = f(G.kd[:, m], k_tok1[:, j, hq * P:(hq + 1) * P], ACT.Copy, scale=edge[:, j, d * 16 + v:d * 16 + v + 1])
                        if m == 3:
                            own(ins.then_inc(G.s_kd, 1), G.s_kd)
                        else:
                            link(ins)

                def negw(n, s):
                    G, k = gset[s], n % 4
                    if k > 0:
                        act.wait_ge(G.s_wt, n // 4 * 3 + k)
                        act.wait_ge(G.s_dy, 6 * n + 6)
                        own(f(G.nw.rearrange("p a b -> p (a b)"), G.flat(2), ACT.Copy, scale=-1.0).then_inc(G.s_nw, 1), G.s_nw)

                act.wait_ge(S["edge"], 2)
                act.wait_ge(S["beta_up"], 1)
                for n in range(16):
                    for s in range(2):
                        exps(n, s)
                    for b in range(1, LEV):
                        for s in range(2):
                            wcopy(n, s, b)
                            if b == 2:
                                values(n, s)
                    for s in range(2):
                        kdecay(n, s)
                    for s in range(2):
                        negw(n, s)

            act.wait_ge(s_in, 64)
            act.wait_ge(S["eps_set"], 1)
            own(f(csilu, cl("c", 0, 16).rearrange("p (a b) -> p a b", b=2), ACT.Silu).then_inc(S["c_ready"], 1), S["c_ready"])
            act.wait_ge(S["rows_copied"], 1)
            link(f(a_exp[:, 0:32], row_bc[:, 32:64], ACT.Exp))
            link(f(a_exp[:, 32:64], row_bc[:, ROWV["alog1"]:ROWV["alog1"] + 32], ACT.Exp))
            modulation0()
            norm("mix0")
            conv_stage("xbc")
            b = out_of("small0", 0, 1)
            act.wait_ge(s_done, b + 1)
            f(glT[0:2 * RANK, :], psum[0:2 * RANK, b % 4, :], ACT.Copy).then_inc(s_drained[b % 4], 1)
            act.wait_ge(s_drained[b % 4], b // 4 + 1)
            own(f(stat[:, 0:1], stat[:, 0:1], ACT.Copy).then_inc(S["gl_ready"], 1), S["gl_ready"])
            act.wait_ge(S["dt_raw"], 1)
            log1p_exp_neg_abs(tmp128, dt, S["dt_ln"])
            for g in range(4):
                for i in range(2):
                    b = out_of("z0", g, i)
                    act.wait_ge(s_done, b + 1)
                    f(z0[:, 2 * i:2 * i + 2, g * CB:(g + 1) * CB], psum[:, b % 4, :].rearrange("p (a b) -> p a b", a=2), ACT.Silu).then_inc(s_drained[b % 4], 1)
                    act.wait_ge(s_drained[b % 4], b // 4 + 1)
            ssd()
            act.dma_start(gate, gate_in).then_inc(s_gate, 16)
            gla()
            norm("ffn0")
            ffn(0)
            norm("mix1")
            gdn_inputs()
            conv_stage("qkv")
            z_and_l2()
            gdn()
            act.wait_ge(S["summed"], 3)
            for i in range(2):
                for h in range(V_H):
                    link(f(ws[:, 0:P], o1[:, i, h * P:(h + 1) * P], ACT.Square, accum_out=stat[:, i * 16 + h:i * 16 + h + 1]))
            link(f(stat[:, 0:32], stat[:, 0:32], ACT.Ln, scale=1.0 / GDN_DV, bias=eps_col[:, 0:1]))
            own(f(stat[:, 0:32], stat[:, 0:32], ACT.Exp, scale=-0.5).then_inc(S["mix_rs"], 1), S["mix_rs"])
            mixed("gdn", 16, 0, lambda t: cl("gdn_norm"), mixT1, LAT)
            norm("ffn1")
            ffn(1)
            norm("fin")

        @block.vector
        def _(dve):
            link, own = in_order(dve, steps["dve"])
            V = nc.vector

            def tt(o, a, b, op):
                return V.tensor_tensor(o, a, b, op)

            def stt(o, a, sc, b, op0, op1):
                return V.scalar_tensor_tensor(out=o, in0=a, scalar=sc, in1=b, op0=op0, op1=op1)

            def ts(o, a, s1, s2, op0, op1=None):
                return V.tensor_scalar(o, a, s1, s2, op0, op1) if op1 else V.tensor_scalar(o, a, s1, None, op0)

            def copy(o, a):
                return V.tensor_copy(o, a)

            def bc(a, axis, n):
                sh = list(a.shape)
                sh.insert(axis, n)
                return a.unsqueeze(axis).to_broadcast(sh)

            def gains(i):
                link(stt(gain[:, i, 0], mod[:, i, 8:16], 1.0, bc(cl("norm_mix", i * KC, KC), 2, 2), ALU.add, ALU.mult))
                link(stt(gain[:, i, 1], mod[:, i, 32:40], 1.0, bc(cl("norm_ffn", i * KC, KC), 2, 2), ALU.add, ALU.mult))

            def modulation0():
                dve.wait_ge(S["mod_columns"], 1)
                link(tt(mod[:, 0], psum[:, 4, 0:96].rearrange("p (a b) -> p a b", b=2), bc(cl("mod_b", 0, 48), 2, 2), ALU.add))
                gains(0)

            def mod1_taken(q):
                dve.wait_ge(S["mod_columns"], q + 2)
                own(tt(mod[:, 1, 4 * q:4 * q + 4], psum[:, 3, 0:8].rearrange("p (a b) -> p a b", b=2),
                       bc(cl("mod_b", 48 + 4 * q, 4), 2, 2), ALU.add).then_inc(S["mod_taken"], 1), S["mod_taken"])

            def norm(tag):
                i, which, s_lo = NORMS[tag]
                dve.wait_ge(S["rs"], NORM_AT[tag][0] + 1)
                for c in range(KC):
                    for s in range(s_lo, 2):
                        x, r, h = xT[:, c, seg(s)], wide[:, 2, seg(s)], hT[:, c, seg(s)]
                        if tag == "fin":
                            own(stt(x, x, cl("final", c), r, ALU.mult, ALU.mult).then_inc(S["final_ready"], 1), S["final_ready"])
                            continue
                        if tag == "mix1" and s == 1:
                            x, r = (a.rearrange("p (r w) -> p r w", w=GRID_W) for a in (x, r))
                            h = h.rearrange("p (w r) -> p r w", r=ROWS)
                        own(stt(h, x, gain[:, i, which, c, s:s + 1], r, ALU.mult, ALU.mult).then_inc(S["scaled"], 1), S["scaled"])

            def conv_stage(stage):
                C = conv_sems[stage]
                info = CONVS[stage]

                def evac(t):
                    n = transposed(stage, t)
                    if n is None:
                        return
                    dve.wait_ge(C["tr"], n + 1)
                    src = psum[:, 6 + n % 2, :].rearrange("p (a b) -> p a b", a=TT)
                    if stage == "xbc":
                        dest = x0[:, :, t * P:(t + 1) * P] if t < 8 else b_tok[:, :, (t - 8) * P:(t - 7) * P]
                    else:
                        dest = v1[:, :, n * P:(n + 1) * P]
                    own(copy(dest, src).then_inc(C["tr_taken"], 1), C["tr_taken"])

                own(V.memset(ws[:, 0:1040], 0.0).then_inc(C["padded"], 1), C["padded"])
                for t in range(info["tiles"]):
                    drained(dve, out_of(stage, t // 2, t % 2))
                    if t - 1 > 0:
                        dve.wait_ge(C["silu"], t - 1)
                    s0, s1 = segs(stage, t)[0], segs(stage, t)[-1] + 1
                    o = conv[:, t % 2, s0 * CTX:T].rearrange("p (s t) -> p s t", t=CTX)
                    for k in range(TAPS):
                        a = raw[:, t % 2, s0:s1, k:k + CTX]
                        wk = cl(info["w"], t * TAPS + k)
                        if k == 0 and stage == "xbc":
                            link(ts(o, a, wk, cl("conv_b0", t), ALU.mult, ALU.add))
                        elif k == 0:
                            link(ts(o, a, wk, None, ALU.mult))
                        else:
                            ins = stt(o, a, wk, o, ALU.mult, ALU.add)
                            if k == TAPS - 1:
                                own(ins.then_inc(C["conv"], 1), C["conv"])
                            else:
                                link(ins)
                    if t >= 2:
                        evac(t - 2)
                evac(info["tiles"] - 2)
                evac(info["tiles"] - 1)

            def ssd():
                for h in range(SSD_H):
                    sl = slice(h * SSD_P, (h + 1) * SSD_P)
                    link(ts(y0[:, :, sl], x0[:, :, sl], row_bc[:, ROWV["dskip"] + h:ROWV["dskip"] + h + 1], None, ALU.mult))
                dve.wait_ge(S["ssd_bc"], 1)
                for g in range(SSD_G):
                    for d in DIRS:
                        own(tt(g_mask[:, d, g], psum[:, 5 + g, :].rearrange("p (a b) -> p a b", a=TT), bc(upto_incl[d], 1, TT), ALU.mult).then_inc(S["ssd_masked"], 1), S["ssd_masked"])
                dve.wait_ge(S["edge"], 1)

                def inputs(d, k):
                    j = TILE_AT[d][k]
                    xj = x0[:, j].rearrange("p (h c) -> p h c", c=SSD_P)
                    link(tt(xdt, xj, bc(dt[:, j, d * 16:d * 16 + 16], 2, SSD_P), ALU.mult))
                    own(tt(xw, xdt, bc(edge[:, j, d * 16:d * 16 + 16], 2, SSD_P), ALU.mult).then_inc(S["ssd_x"], 1), S["ssd_x"])

                def accumulate(v):
                    d, k, g = v // 8, v // 2 % 4, v % 2
                    j = TILE_AT[d][k]
                    y = y0[:, j, g * 512:(g + 1) * 512]
                    dve.wait_ge(S["ssd_pair"], v + 1)

                    def per_head(a):
                        return a.rearrange("p (h c) -> p h c", c=SSD_P)
                    if k > 0:
                        link(tt(per_head(ytmp), per_head(psum[:, 2 + v % 2, :]),
                           bc(edge[:, j, 32 + d * 16 + g * 8:40 + d * 16 + g * 8], 2, SSD_P), ALU.mult))
                        link(tt(y, y, ytmp, ALU.add))
                    link(tt(y, y, psum[:, 6 + v % 2, :], ALU.add))
                    if k == 0:
                        own(copy(st0[:, g], psum[:, v % 2, :]).then_inc(S["ssd_y"], 1), S["ssd_y"])
                    else:
                        link(tt(per_head(st0[:, g]), per_head(st0[:, g]),
                           bc(edge[:, j, 64 + d * 16 + g * 8:72 + d * 16 + g * 8], 2, SSD_P), ALU.mult))
                        own(tt(st0[:, g], st0[:, g], psum[:, v % 2, :], ALU.add).then_inc(S["ssd_y"], 1), S["ssd_y"])

                for u in range(32):
                    d, k, g, hq = u // 16, u // 4 % 4, u // 2 % 2, u % 2
                    if u % 4 == 0:
                        if u > 0:
                            accumulate(u // 2 - 1)
                        inputs(d, k)
                    dve.wait_ge(S["ssd_exp"], u + 1)
                    if u - 1 > 0:
                        dve.wait_ge(S["ssd_diag"], u - 1)
                    own(tt(p_seg[:, u % 2], e_seg[:, u % 2], bc(g_mask[:, d, g, TILE_AT[d][k]], 1, 4), ALU.mult).then_inc(S["ssd_p"], 1), S["ssd_p"])
                    if u % 4 == 3:
                        accumulate(u // 2 - 1)
                accumulate(15)
                own(tt(y0, y0, z0, ALU.mult).then_inc(S["summed"], 1), S["summed"])
                dve.wait_ge(S["mix_rs"], 1)
                for j in range(TT):
                    for g in range(SSD_G):
                        y = y0[:, j, g * 512:(g + 1) * 512]
                        ins = ts(y, y, stat[:, j * 2 + g:j * 2 + g + 1], None, ALU.mult)
                        if j == TT - 1 and g == 1:
                            own(ins.then_inc(S["merged"], 1), S["merged"])
                        else:
                            link(ins)

            def gla():
                for j in range(TT):
                    dve.wait_ge(S["gk_ln"], j + 1)
                    own(stt(gk[:, j], psum[:, 4:6, :], 0.0, gtmp.rearrange("p (a b) -> p a b", a=2), ALU.min, ALU.subtract).then_inc(S["gk"], 1), S["gk"])
                for h in range(GLA_H):
                    dve.wait_ge(S["k_tr"], h + 1)
                    own(copy(k_tok0[:, :, h * P:(h + 1) * P], psum[:, 6 + h % 2, :].rearrange("p (a b) -> p a b", a=TT)).then_inc(S["k_tok"], 1), S["k_tok"])

                def weigh(w):
                    d, k, h = w // 16, w // 4 % 4, w % 4
                    j = TILE_AT[d][k]
                    dve.wait_ge(S["gla_exp"], w + 1)
                    for b in range(LEV):
                        for half in range(2):
                            src = (q0 if half != d else k0)[:, h, j * P:(j + 1) * P]
                            o, e, a = (t.rearrange("p (k h i) -> p k h i", h=2, i=1 << b)[:, :, half, :]
                                       for t in (qk[:, w % 2, b], el[:, w % 2, b], src))
                            link(tt(o, e, a, ALU.mult))
                    end = (P - 1, 0)[d]
                    link(copy(tile_decay[:, w % 3:w % 3 + 1], el[:, w % 2, LEV, end:end + 1]))
                    own(tt(q_in[:, w % 3], el[:, w % 2, LEV], q0[:, h, j * P:(j + 1) * P], ALU.mult).then_inc(S["gla_qk"], 1), S["gla_qk"])

                def taken(w):
                    d, k, h = w // 16, w // 4 % 4, w % 4
                    j = TILE_AT[d][k]
                    dve.wait_ge(S["gla_out"], w + 1)
                    o = o0[:, j, h * GLA_DV:(h + 1) * GLA_DV]
                    if d == 0:
                        link(copy(o, psum[:, 1, 0:GLA_DV]))
                    else:
                        link(tt(o, o, psum[:, 1, 0:GLA_DV], ALU.add))
                    if k == 0:
                        own(copy(st_gla[:, h], psum[:, 2, 0:GLA_DV]).then_inc(S["gla_taken"], 1), S["gla_taken"])
                    else:
                        own(stt(st_gla[:, h], st_gla[:, h], tile_decay[:, w % 3:w % 3 + 1], psum[:, 2, 0:GLA_DV], ALU.mult, ALU.add).then_inc(S["gla_taken"], 1), S["gla_taken"])

                def attention(w):
                    d, k, h = w // 16, w // 4 % 4, w % 4
                    j = TILE_AT[d][k]
                    dve.wait_ge(S["gla_scores"], w + 1)
                    own(tt(am[:, :, :], psum[:, 6:8, :].rearrange("p a (b c) -> p (a b) c", c=P), cms(f"msk{d}", 8), ALU.mult).then_inc(S["gla_masked"], 1), S["gla_masked"])
                    if w - 1 > 0:
                        dve.wait_ge(S["gla_out"], w - 1)
                    own(V.tensor_reduce(att0[:, w % 2], am[:, :, :].rearrange("p b l -> p l b"), AX_X, ALU.add).then_inc(S["gla_att"], 1), S["gla_att"])
                    if h == 0:
                        dve.wait_ge(S["gla_kexp"], w // 4 + 1)
                        own(tt(kdec0[:, w // 4 % 2], kdec0[:, w // 4 % 2], k_tok0[:, j, :], ALU.mult).then_inc(S["gla_kdec"], 1), S["gla_kdec"])

                weigh(0)
                for w in range(32):
                    if w % 2 == 0 and 0 < w <= 24:
                        mod1_taken(w // 2 - 1)
                    if w + 1 < 32:
                        weigh(w + 1)
                    attention(w)
                    if w > 0:
                        taken(w - 1)
                taken(31)
                gains(1)
                own(copy(stat[:, 30:31], stat[:, 30:31]).then_inc(S["summed"], 1), S["summed"])
                dve.wait_ge(S["mix_rs"], 2)
                for j in range(TT):
                    for h in range(GLA_H):
                        o = o0[:, j, h * GLA_DV:(h + 1) * GLA_DV]
                        ins = stt(o, o, stat[:, j * 4 + h:j * 4 + h + 1], r0[:, j, h * GLA_DV:(h + 1) * GLA_DV], ALU.mult, ALU.mult)
                        if j == TT - 1 and h == GLA_H - 1:
                            own(ins.then_inc(S["merged"], 1), S["merged"])
                        else:
                            link(ins)

            def residual(stage, i, which):
                for t in range(KC):
                    b = out_of(stage, t // 2, t % 2)
                    dve.wait_ge(s_done, b + 1)
                    for s in range(i, 2):
                        x, y = xT[:, t, seg(s)], psum[:, b % 4, seg(s)]
                        if stage == "out1":
                            x = x.rearrange("p (r w) -> p r w", w=GRID_W)
                            y = y.rearrange("p (w r) -> p r w", r=ROWS)
                        ins = stt(x, y, mod[:, i, 16 + 24 * which + t, s:s + 1], x, ALU.mult, ALU.add)
                        if s == 1:
                            ins.then_inc(s_drained[b % 4], 1)
                            dve.wait_ge(s_drained[b % 4], b // 4 + 1)
                        else:
                            link(ins)
                    own(ts(stat[:, 31:32], stat[:, 31:32], 0.0, None, ALU.mult).then_inc(S["residual"], 1), S["residual"])

            def ffn(i):
                lo = i * CTX
                for g in range(D_FF // CB):
                    for ff in range(2):
                        t = 2 * g + ff
                        drained(dve, out_of(f"ff{i}", 2 * g, ff))
                        b = out_of(f"ff{i}", 2 * g + 1, ff)
                        dve.wait_ge(s_done, b + 1)
                        tt(hidden[:, t, lo:T], gate_act[:, t % 4, lo:T], psum[:, b % 4, lo:T], ALU.mult).then_inc(s_drained[b % 4], 1)
                        dve.wait_ge(s_drained[b % 4], b // 4 + 1)
                        own(ts(stat[:, 31:32], stat[:, 31:32], 0.0, None, ALU.mult).then_inc(S["hidden"], 1), S["hidden"])
                residual(f"dn{i}", i, 1)

            def gdn():
                def products(n, s):
                    G, hq, k = gset[s], 2 * (n // 4) + s, n % 4
                    dve.wait_ge(G.s_ea, n + 1)
                    for m in range(4):
                        d, v = m // 2, 2 * hq + m % 2
                        j = TILE_AT[d][k]
                        ins = stt(G.a[:, d, m % 2], G.ea[:, d, m % 2], beta[:, j, d * 16 + v:d * 16 + v + 1], G.bank(2)[:, d], ALU.mult, ALU.mult)
                        if m == 3:
                            own(ins.then_inc(G.s_a, 1), G.s_a)
                        else:
                            link(ins)
                    if k >= 2:
                        dve.wait_ge(G.s_et, n // 4 * 2 + k - 1)
                        for d in DIRS:
                            own(tt(G.att[:, d], G.att[:, d], bc(G.bank(2)[:, 2 + d], 1, 2), ALU.mult).then_inc(G.s_raw, 1), G.s_raw)
                    dve.wait_ge(G.s_level, 7 * n + 1)
                    link(tt(G.x, bc(ident, 1, 4), G.level.rearrange("p a b c -> p (a b) c"), ALU.subtract))

                def first_y(n, s):
                    G = gset[s]
                    dve.wait_ge(G.s_w, 7 * n + 1)
                    own(tt(G.y, bc(ident, 1, 4), G.bank(0), ALU.subtract).then_inc(G.s_inv, 1), G.s_inv)

                def update(n, s, b):
                    G = gset[s]
                    dve.wait_ge(G.s_dy, 6 * n + b)
                    ins = tt(G.y, G.y, G.bank(0), ALU.subtract)
                    if b == LEV - 1:
                        own(ins.then_inc(G.s_inv, 1), G.s_inv)
                    else:
                        link(ins)
                    if b < LEV - 1:
                        dve.wait_ge(G.s_dx, 5 * n + b)
                        own(tt(G.x, G.x, G.bank(1), ALU.subtract).then_inc(G.s_inv, 1), G.s_inv)

                def vcopy(n, s):
                    G = gset[s]
                    dve.wait_ge(G.s_new, n + 1)
                    own(copy(G.vn, G.bank(3)).then_inc(G.s_vn, 1), G.s_vn)

                def collect(n, s):
                    G, hq, k = gset[s], 2 * (n // 4) + s, n % 4
                    dve.wait_ge(G.s_out, n + 1)
                    if k >= 2:
                        for m in range(4):
                            d, v = m // 2, 2 * hq + m % 2
                            j = TILE_AT[d][k]
                            o = o1[:, j - 2, v * P:(v + 1) * P]
                            link(stt(o, G.bank(0)[:, m], edge[:, j, 32 + d * 16 + v:33 + d * 16 + v], o, ALU.mult, ALU.add))
                        for d in DIRS:
                            o = o1[:, TILE_AT[d][k] - 2, 2 * hq * P:(2 * hq + 2) * P]
                            ins = tt(o, o, G.flat(1)[:, d * 256:(d + 1) * 256], ALU.add)
                            if k == 3 and d == 1:
                                own(ins.then_inc(G.s_end, 1), G.s_end)
                            else:
                                link(ins)
                    if k == 0:
                        own(copy(G.s, G.bank(2)).then_inc(G.s_end, 1), G.s_end)
                    elif k < 3:
                        for m in range(4):
                            d, v = m // 2, 2 * hq + m % 2
                            j = TILE_AT[d][k]
                            ins = stt(G.s[:, m], G.s[:, m], edge[:, j, 64 + d * 16 + v:65 + d * 16 + v], G.bank(2)[:, m], ALU.mult, ALU.add)
                            if m == 3:
                                own(ins.then_inc(G.s_end, 1), G.s_end)
                            else:
                                link(ins)

                for n in range(16):
                    for s in range(2):
                        products(n, s)
                    for s in range(2):
                        first_y(n, s)
                    for b in range(1, LEV):
                        for s in range(2):
                            update(n, s, b)
                    for s in range(2):
                        vcopy(n, s)
                    for s in range(2):
                        collect(n, s)

            own(V.memset(psum[:, 0:4, :], 0.0).then_inc(S["banks_zeroed"], 1), S["banks_zeroed"])
            link(V.memset(eps_col[:, 0:1], EPS))
            own(V.memset(eps_col[:, 1:2], float(np.log(GDN_DK ** -0.5))).then_inc(S["eps_set"], 1), S["eps_set"])
            link(V.memset(stat, 1.0))
            dve.wait_ge(S["rows_spread"], 1)
            own(copy(row_bc, psum[:, 7, 0:NROW]).then_inc(S["rows_copied"], 1), S["rows_copied"])
            modulation0()
            link(V.memset(glT[2 * RANK:2 * RANK + 1, :], 1.0))
            norm("mix0")
            conv_stage("xbc")
            b = out_of("small0", 0)
            dve.wait_ge(s_done, b + 1)
            tt(dt, psum[:, b % 4, 0:128].rearrange("p (a b) -> p a b", a=TT), bc(row_bc[:, 0:32], 1, TT), ALU.add).then_inc(s_drained[b % 4], 1)
            dve.wait_ge(s_drained[b % 4], b // 4 + 1)
            own(copy(stat[:, 31:32], stat[:, 31:32]).then_inc(S["dt_raw"], 1), S["dt_raw"])
            dve.wait_ge(S["dt_ln"], 1)
            link(stt(dt, dt, 0.0, tmp128, ALU.max, ALU.add))
            own(stt(da, dt, -1.0, bc(a_exp[:, 0:32], 1, TT), ALU.mult, ALU.mult).then_inc(S["decay"], 1), S["decay"])
            ssd()
            gla()
            residual("out0", 0, 0)
            norm("ffn0")
            ffn(0)
            norm("mix1")
            b = out_of("small1", 0)
            dve.wait_ge(s_done, b + 1)
            ps = psum[:, b % 4, 0:256].rearrange("p (a b) -> p a b", a=TT)
            link(tt(small_ab[:, :, 0:32], ps[:, :, 0:32], bc(row_bc[:, ROWV["dtb1"]:ROWV["dtb1"] + 32], 1, TT), ALU.add))
            copy(small_ab[:, :, 32:64], ps[:, :, 32:64]).then_inc(s_drained[b % 4], 1)
            dve.wait_ge(s_drained[b % 4], b // 4 + 1)
            own(copy(stat[:, 31:32], stat[:, 31:32]).then_inc(S["ab_raw"], 1), S["ab_raw"])
            dve.wait_ge(S["ab_ln"], 1)
            link(stt(da, small_ab[:, :, 0:32], 0.0, tmp128, ALU.max, ALU.add))
            own(stt(da, da, -1.0, bc(a_exp[:, 32:64], 1, TT), ALU.mult, ALU.mult).then_inc(S["decay"], 1), S["decay"])
            conv_stage("qkv")
            for t in range(16):
                a = q1[:, t] if t < 8 else k1[:, t - 8]
                dve.wait_ge(S["l2_rs"], t + 1)
                own(tt(a, a, rs_q[:, t] if t < 8 else rs_k[:, t - 8], ALU.mult).then_inc(S["l2_mul"], 1), S["l2_mul"])
            for h in range(QK_H):
                dve.wait_ge(S["k_tr1"], h + 1)
                own(copy(k_tok1[:, :, h * P:(h + 1) * P], psum[:, 6 + h % 2, :].rearrange("p (a b) -> p a b", a=TT)).then_inc(S["k_tok1"], 1), S["k_tok1"])
            dve.wait_ge(S["edge"], 2)
            own(tt(beta_up, beta, edge[:, :, 32:64], ALU.mult).then_inc(S["beta_up"], 1), S["beta_up"])
            link(V.memset(hT[:, :, :].rearrange("p a b -> p (a b)"), 0.0))
            gdn()
            own(copy(stat[:, 31:32], stat[:, 31:32]).then_inc(S["summed"], 1), S["summed"])
            dve.wait_ge(S["mix_rs"], 3)
            for i in range(2):
                for h in range(V_H):
                    o = o1[:, i, h * P:(h + 1) * P]
                    ins = stt(o, o, stat[:, i * 16 + h:i * 16 + h + 1], z1[:, i, h * P:(h + 1) * P], ALU.mult, ALU.mult)
                    if i == 1 and h == V_H - 1:
                        own(ins.then_inc(S["merged"], 1), S["merged"])
                    else:
                        link(ins)
            residual("out1", 1, 0)
            norm("ffn1")
            ffn(1)
            norm("fin")

        @block.gpsimd
        def _(pool):
            link, own = in_order(pool, steps["pool"])
            G_ = nc.gpsimd

            def tt(o, a, b):
                return G_.tensor_tensor(o, a, b, ALU.mult)

            def bc(a, axis, n):
                sh = list(a.shape)
                sh.insert(axis, n)
                return a.unsqueeze(axis).to_broadcast(sh)

            pool.wait_ge(S["decay"], 1)
            pool.wait_ge(conv_sems["xbc"]["tr_taken"], 10)
            for u in range(32):
                d, k, g, hq = u // 16, u // 4 % 4, u // 2 % 2, u % 2
                at = d * 16 + g * 8 + hq * 4
                if u - 1 > 0:
                    pool.wait_ge(S["ssd_seg"], u - 1)
                own(tt(g_decay[:, u % 2], bc(da[:, TILE_AT[d][k], at:at + 4], 2, P), bc(upto_incl[d], 1, 4)).then_inc(S["ssd_r"], 1), S["ssd_r"])
            pool.wait_ge(S["beta_up"], 1)
            for n in range(16):
                for s in range(2):
                    G, hq, k = gset[s], 2 * (n // 4) + s, n % 4
                    if 5 * n > 0:
                        pool.wait_ge(G.s_dx, 5 * n)
                    if 6 * n > 0:
                        pool.wait_ge(G.s_dy, 6 * n)
                    for d in DIRS:
                        j = TILE_AT[d][k]
                        at = d * 16 + 2 * hq
                        ins = tt(G.decay[:, d], bc(da[:, j, at:at + 2], 2, P), bc(upto_incl[d], 1, 2))
                        if d == 1:
                            own(ins.then_inc(G.s_decay, 1), G.s_decay)
                        else:
                            link(ins)
                for b in range(LEV):
                    for s in range(2):
                        G, k = gset[s], n % 4
                        if b == 0:
                            pool.wait_ge(G.s_a, n + 1)
                            if n > 0:
                                pool.wait_ge(G.s_out, n)
                        else:
                            pool.wait_ge(G.s_w, 7 * n + b)
                            if b == 1:
                                pool.wait_ge(G.s_inv, 7 * n + 1)
                        for d in DIRS:
                            ins = tt(G.level[:, d], G.a[:, d], bc(cm(f"msk{1 - d}", b), 1, 2))
                            if d == 1:
                                own(ins.then_inc(G.s_level, 1), G.s_level)
                            else:
                                link(ins)
                        if b == 0 and k >= 2:
                            pool.wait_ge(G.s_raw, 2 * (n // 4 * 2 + k - 1))
                            for d in DIRS:
                                ins = tt(G.att[:, d], G.att[:, d], bc(upto_incl[d], 1, 2))
                                if d == 1:
                                    own(ins.then_inc(G.s_att, 1), G.s_att)
                                else:
                                    link(ins)


def kernel(**inputs):
    import concourse.bacc as bacc
    from concourse.bass_utils import run_bass_kernel_spmd

    w = {n: np.asarray(a) for n, a in inputs.items()}
    xT = np.concatenate([w["ctx"][0], w["x"][0]]).T.reshape(KC, P, T).transpose(1, 0, 2).reshape(P, -1)
    arrays = {"x": xT, "w": pack_weights(w), "cols": pack_columns(w), "rows": pack_rows(w),
              "gate": pack_gate(w), "consts": constants().reshape(P, -1)}
    arrays = {n: np.ascontiguousarray(a) for n, a in arrays.items()}
    nc = bacc.Bacc("TRN2", target_bir_lowering=False, num_devices=1)
    aps = [nc.dram_tensor(n, a.shape, mybir.dt.from_np(a.dtype), kind="ExternalInput").ap() for n, a in arrays.items()]
    o = nc.dram_tensor("y", (P, KC * LAT), F32, kind="ExternalOutput").ap()
    backbone(nc, *aps, o)
    r = run_bass_kernel_spmd(nc, [arrays], core_ids=[0])
    y = np.asarray(r.results[0]["y"])
    return np.ascontiguousarray(y.reshape(P, KC, LAT).transpose(2, 1, 0)).reshape(1, LAT, D)
```
